# Optimizing a Trainium2 kernel written in Bass

```python
import math
import jax, jax.numpy as jnp
from jax import lax
import numpy as np

D_MODEL = 2048
BATCH = 1
SEQ = 256
DEPTH = 1

N_META = 16
D_CONV = D_MODEL
CONV_W = 3
CONV_GROUPS = 8
MLSTM_HEADS = 8
D_MV = D_MODEL
D_MQK = D_MODEL // 2
HEAD_V = D_MV // MLSTM_HEADS
HEAD_QK = D_MQK // MLSTM_HEADS
CHUNK = 64
PEER_HEADS = 8
N_KEYS = 128
N_EXPERTS = N_KEYS * N_KEYS
D_KEY = 256
HALF_KEY = D_KEY // 2
TOPK = 16
PEER_BLOCK = 128
N_IN = 3 * D_CONV + 2 * D_MQK + 2 * D_MV + 2 * MLSTM_HEADS + 2 * D_MODEL
ALPHA = (2 * DEPTH) ** 0.25
BETA = (8 * DEPTH) ** -0.25
LN_EPS = 1e-5
I_GATE_PAD = -1e30

kernel_name = "hybrid_conv_mlstm_peer_block"

def layer_norm(x, g, b):
    xf = x.astype(jnp.float32)
    mu = xf.mean(-1, keepdims=True)
    var = jnp.square(xf - mu).mean(-1, keepdims=True)
    y = (xf - mu) * lax.rsqrt(var + LN_EPS)
    return (y * g + b).astype(x.dtype)

def short_conv_mixer(b_gate, c_gate, xc, conv_w):
    z = c_gate * xc
    L = z.shape[1]
    zp = jnp.pad(z, ((0, 0), (CONV_W - 1, 0), (0, 0)))
    y = sum(conv_w[k] * zp[:, k:k + L] for k in range(CONV_W))
    return b_gate * y

def mlstm_chunkwise(q, k, v, i_pre, f_pre):
    Bsz, L = q.shape[:2]
    pad = (-L) % CHUNK

    def lead_pad(a, value=0.0):
        return jnp.pad(a, ((0, 0), (pad, 0)) + ((0, 0),) * (a.ndim - 2), constant_values=value)

    q = lead_pad(q.astype(jnp.float32) * (HEAD_QK ** -0.5))
    k = lead_pad(k.astype(jnp.float32))
    v = lead_pad(v.astype(jnp.float32))
    log_i = lead_pad(i_pre.astype(jnp.float32), I_GATE_PAD)
    log_f = lead_pad(jax.nn.log_sigmoid(f_pre.astype(jnp.float32)))
    Lp = L + pad
    nc = Lp // CHUNK

    def to_chunks(a):
        a = a.reshape((Bsz, nc, CHUNK) + a.shape[2:])
        return jnp.moveaxis(a, (1, 3), (0, 2))

    xs = (to_chunks(q), to_chunks(k), to_chunks(v), to_chunks(log_i), to_chunks(log_f))
    causal = jnp.tril(jnp.ones((CHUNK, CHUNK), dtype=bool))

    def step(carry, xs_c):
        C, n, m = carry
        qc, kc, vc, li, lf = xs_c
        b = jnp.cumsum(lf, axis=-1)
        d = b[..., :, None] - b[..., None, :] + li[..., None, :]
        d = jnp.where(causal, d, -jnp.inf)
        inter = b + m[..., None]
        m_t = jnp.maximum(inter, d.max(-1))
        w = jnp.exp(d - m_t[..., None])
        s = jnp.einsum('bhtd,bhsd->bhts', qc, kc) * w
        sc_inter = jnp.exp(inter - m_t)
        num = (jnp.einsum('bhts,bhsv->bhtv', s, vc)
               + sc_inter[..., None] * jnp.einsum('bhtd,bhdv->bhtv', qc, C))
        den = s.sum(-1) + sc_inter * jnp.einsum('bhtd,bhd->bht', qc, n)
        h = num / jnp.maximum(jnp.abs(den), jnp.exp(-m_t))[..., None]
        b_last = b[..., -1]
        dl = b_last[..., None] - b + li
        m_new = jnp.maximum(b_last + m, dl.max(-1))
        wl = jnp.exp(dl - m_new[..., None])
        decay = jnp.exp(b_last + m - m_new)
        C_new = decay[..., None, None] * C + jnp.einsum('bhs,bhsd,bhsv->bhdv', wl, kc, vc)
        n_new = decay[..., None] * n + jnp.einsum('bhs,bhsd->bhd', wl, kc)
        return (C_new, n_new, m_new), h

    H = q.shape[2]
    init = (jnp.zeros((Bsz, H, HEAD_QK, HEAD_V), jnp.float32),
            jnp.zeros((Bsz, H, HEAD_QK), jnp.float32),
            jnp.zeros((Bsz, H), jnp.float32))
    _, hs = lax.scan(step, init, xs)
    hs = jnp.transpose(hs, (1, 0, 3, 2, 4)).reshape(Bsz, Lp, H, HEAD_V)
    return hs[:, pad:]

def token_mixer(h, w_in, b_if, conv_w, mh_norm_w, p_a, p_b, w_o):
    Bsz, L, _ = h.shape
    proj = jnp.einsum('bld,dn->bln', h, w_in)
    sizes = [D_CONV, D_CONV, D_CONV, D_MQK, D_MQK, D_MV, D_MV, 2 * MLSTM_HEADS, D_MODEL, D_MODEL]
    offsets = np.cumsum(sizes)[:-1].tolist()
    cb, cc, cx, q, k, v, o, gif, ga, gb = jnp.split(proj, offsets, axis=-1)
    y_a = short_conv_mixer(cb, cc, cx, conv_w)
    i_pre = gif[..., :MLSTM_HEADS] + b_if[:MLSTM_HEADS]
    f_pre = gif[..., MLSTM_HEADS:] + b_if[MLSTM_HEADS:]
    hm = mlstm_chunkwise(q.reshape(Bsz, L, MLSTM_HEADS, HEAD_QK),
                         k.reshape(Bsz, L, MLSTM_HEADS, HEAD_QK),
                         v.reshape(Bsz, L, MLSTM_HEADS, HEAD_V), i_pre, f_pre)
    hm = hm * lax.rsqrt(jnp.mean(jnp.square(hm), -1, keepdims=True) + LN_EPS)
    hm = hm.reshape(Bsz, L, D_MV) * mh_norm_w
    y_b = jax.nn.sigmoid(o) * hm.astype(h.dtype)
    merged = (jax.nn.sigmoid(ga) * jnp.einsum('blc,cd->bld', y_a, p_a)
              + jax.nn.sigmoid(gb) * jnp.einsum('blc,cd->bld', y_b, p_b))
    return jnp.einsum('bld,de->ble', merged, w_o)

def peer_ffn(h, peer_wq, peer_keys, peer_u, peer_v):
    Bsz, L, D = h.shape
    T = Bsz * L
    t = h.reshape(T, D)
    q = (t @ peer_wq).reshape(T, PEER_HEADS, 2, HALF_KEY)
    sc = jnp.einsum('thpk,hpnk->thpn', q, peer_keys).astype(jnp.float32)
    s_top, i_top = lax.top_k(sc, TOPK)
    cand = s_top[..., 0, :, None] + s_top[..., 1, None, :]
    cand_idx = i_top[..., 0, :, None] * N_KEYS + i_top[..., 1, None, :]
    best_s, best_pos = lax.top_k(cand.reshape(T, PEER_HEADS, TOPK * TOPK), TOPK)
    expert_idx = jnp.take_along_axis(cand_idx.reshape(T, PEER_HEADS, TOPK * TOPK), best_pos, axis=-1)
    g = jax.nn.softmax(best_s, axis=-1)
    idx = expert_idx.reshape(T, PEER_HEADS * TOPK)
    g = g.reshape(T, PEER_HEADS * TOPK).astype(h.dtype)
    npad = (-T) % PEER_BLOCK
    tb = jnp.pad(t, ((0, npad), (0, 0))).reshape(-1, PEER_BLOCK, D)
    ib = jnp.pad(idx, ((0, npad), (0, 0))).reshape(-1, PEER_BLOCK, PEER_HEADS * TOPK)
    gbk = jnp.pad(g, ((0, npad), (0, 0))).reshape(-1, PEER_BLOCK, PEER_HEADS * TOPK)

    def eval_block(args):
        xb, eb, wb = args
        u = peer_u[eb]
        a = jax.nn.gelu(jnp.einsum('td,tkd->tk', xb, u), approximate=False)
        return jnp.einsum('tk,tkd->td', wb * a, peer_v[eb])

    out = lax.map(eval_block, (tb, ib, gbk))
    return out.reshape(-1, D)[:T].reshape(Bsz, L, D)

def setup_inputs(seed: int = 0) -> dict:
    key = jax.random.key(seed)
    ks = jax.random.split(key, 24)
    nrm = jax.random.normal
    D = D_MODEL
    H = MLSTM_HEADS
    b_i = 0.1 * nrm(ks[3], (DEPTH, H))
    b_f = jnp.linspace(3.0, 6.0, H)[None, :] + 0.1 * nrm(ks[4], (DEPTH, H))
    return {
        "x": nrm(ks[0], (BATCH, SEQ, D), jnp.float32),
        "meta_tokens": nrm(ks[1], (N_META, D), jnp.float32),
        "ln0_g": 1.0 + 0.1 * nrm(ks[20], (D,)),
        "ln0_b": 0.02 * nrm(ks[21], (D,)),
        "w_in": nrm(ks[2], (DEPTH, D, N_IN)) * D ** -0.5,
        "b_if": jnp.concatenate([b_i, b_f], axis=-1),
        "conv_w": nrm(ks[5], (DEPTH, CONV_W, D_CONV)) * CONV_W ** -0.5,
        "mh_norm_w": 1.0 + 0.1 * nrm(ks[6], (DEPTH, D_MV)),
        "p_a": nrm(ks[7], (DEPTH, D_CONV, D)) * D_CONV ** -0.5,
        "p_b": nrm(ks[8], (DEPTH, D_MV, D)) * D_MV ** -0.5,
        "w_o": nrm(ks[9], (DEPTH, D, D)) * (D ** -0.5) * BETA,
        "ln1_g": 1.0 + 0.1 * nrm(ks[10], (DEPTH, D)),
        "ln1_b": 0.02 * nrm(ks[11], (DEPTH, D)),
        "peer_wq": nrm(ks[12], (DEPTH, D, PEER_HEADS * D_KEY)) * D ** -0.5,
        "peer_keys": nrm(ks[13], (DEPTH, PEER_HEADS, 2, N_KEYS, HALF_KEY)) * HALF_KEY ** -0.5,
        "peer_u": nrm(ks[14], (DEPTH, N_EXPERTS, D)) * D ** -0.5,
        "peer_v": nrm(ks[15], (DEPTH, N_EXPERTS, D)) * BETA,
        "ln2_g": 1.0 + 0.1 * nrm(ks[16], (DEPTH, D)),
        "ln2_b": 0.02 * nrm(ks[17], (DEPTH, D)),
    }

def reference(x, meta_tokens, ln0_g, ln0_b, w_in, b_if, conv_w, mh_norm_w, p_a, p_b, w_o,
              ln1_g, ln1_b, peer_wq, peer_keys, peer_u, peer_v, ln2_g, ln2_b):
    Bsz = x.shape[0]
    meta = jnp.broadcast_to(meta_tokens[None].astype(x.dtype), (Bsz, N_META, D_MODEL))
    h = layer_norm(jnp.concatenate([meta, x], axis=1), ln0_g, ln0_b)
    for l in range(DEPTH):
        mix = token_mixer(h, w_in[l], b_if[l], conv_w[l], mh_norm_w[l], p_a[l], p_b[l], w_o[l])
        h = layer_norm(ALPHA * h + mix, ln1_g[l], ln1_b[l])
        ffn = peer_ffn(h, peer_wq[l], peer_keys[l], peer_u[l], peer_v[l])
        h = layer_norm(ALPHA * h + ffn, ln2_g[l], ln2_b[l])
    return h[:, N_META:]


_drawn_inputs = setup_inputs


def setup_inputs(seed=0):
    import zlib

    import numpy as np

    out = dict(_drawn_inputs(seed))
    spreads = {}
    factors = {'ln2_b': 2.844}
    for name, (base, spread) in spreads.items():
        noise = np.random.default_rng([zlib.crc32(name.encode()), seed]).standard_normal(out[name].shape)
        drawn = base * np.exp(spread * noise) if base else spread * noise
        out[name] = __import__('jax').numpy.asarray(drawn.astype(out[name].dtype))
    for name, factor in factors.items():
        out[name] = (out[name] * factor).astype(out[name].dtype)
    return out
```

```python
from contextlib import ExitStack

import numpy as np
import concourse.bass as bass
from concourse import mybir

F32 = mybir.dt.float32
F32R = mybir.dt.float32r
BF16 = mybir.dt.bfloat16
U32 = mybir.dt.uint32
ALU = mybir.AluOpType
ACT = mybir.ActivationFunctionType
AX = mybir.AxisListType

P = 128
D = 2048
KT = D // P
SEQ, META = 256, 16
L = SEQ + META
NT = SEQ // P
HEADS, HQK, HV = 8, 128, 256
CONV_W = 3
N_GATE = 2 * HEADS
PH, NKEY, TOPK = 8, 128, 16
SLOTS = PH * TOPK
ALPHA = 2 ** 0.25
EPS = 1e-5
QSCALE = HQK ** -0.5
NEG = -3.0e38

C_CB, C_CC, C_CX = 0, D, 2 * D
C_Q = 3 * D
C_K = C_Q + HEADS * HQK
C_V = C_K + HEADS * HQK
C_O = C_V + D
C_GATE = C_O + D
C_GA = C_GATE + N_GATE
C_GB = C_GA + D

NB = 4
GW = NB * P
CHUNKS, HALVES = 4, 8
SLOT_N = 4
AHEAD = 3
G_CONV, G_GA, G_O, G_GB, G_WO, G_WQ = 8, 20, 28, 32, 40, 44
GROUPS = 48

RING = 4


class Steps:

    def __init__(self, eng, sem):
        self.eng, self.sem, self.base, self.k, self.i, self.per = eng, sem, 0, 0, None, 0

    def loop(self, i, per):
        self.base, self.k, self.i, self.per = self.base + self.k, 0, i, per

    def end(self, n):
        assert self.k == self.per, (self.k, self.per)
        self.base, self.k, self.i = self.base + n * self.per, 0, None

    def link(self, ins):
        ins.then_inc(self.sem, 1)
        self.k += 1
        at = self.base + self.k
        self.eng.wait_ge(self.sem, at if self.i is None else self.i * self.per + at)


def decoder_layer(nc, x, meta_tokens, ln0_g, ln0_b, w_in, b_if, conv_w, mh_norm_w, p_a, p_b, w_o,
                  ln1_g, ln1_b, peer_wq, peer_keys, peer_u, peer_v, ln2_g, ln2_b, out):
    w_in, p_a, p_b, w_o, peer_wq = w_in[0], p_a[0], p_b[0], w_o[0], peer_wq[0]
    peer_u, peer_v = peer_u[0], peer_v[0]
    keys_rows = peer_keys[0].rearrange("h p n k -> n (h p) k")

    ctx = ExitStack()
    with ctx:
        top = [-(-nc.sbuf_base // 64) * 64]

        def area(nbytes):
            at = top[0]
            top[0] += -(-nbytes // 64) * 64
            assert top[0] <= nc.sbuf_usable_end, top
            return at

        def sb(name, shape, dt, at=None):
            size = int(np.prod(shape[1:])) * mybir.dt.size(dt)
            return nc.alloc_sbuf_tensor_at(name, shape, dt, offset=area(size) if at is None else at)

        KB = 1024
        a_stream = area(64 * KB)
        a_x = area(2 * KT * L * 4)
        a_y = area(32 * KB)
        a_m = area(32 * KB)
        a_head = area(NB * L * 4 + 10 * KB + 512)
        a_tmp = area(13 * KB)

        ident = sb("ident", [P, P], F32)
        par = sb("par", [P, 8, KT], F32)
        LN0G, LN0B, MHW, LN1G, LN1B, CONV = 0, 1, 2, 3, 4, 5

        raw = sb("raw", [P, CHUNKS, 4, GW], F32, a_stream)
        hi = sb("hi", [P, SLOT_N, 2, GW], F32R, a_stream + 32 * KB)
        lo = sb("lo", [P, SLOT_N, 2, GW], F32R, a_stream + 48 * KB)
        xh = sb("xh", [P, KT, L], F32R, a_x)
        xl = sb("xl", [P, KT, L], F32R, a_x + KT * L * 4)
        yh = sb("yh", [P, KT, SEQ], F32R, a_y)
        yl = sb("yl", [P, KT, SEQ], F32R, a_y + 16 * KB)
        neg_m = sb("neg_m", [P, HEADS, SEQ], F32, a_y + 16 * KB)
        mh = sb("mh", [P, KT, SEQ], F32R, a_m)
        ml = sb("ml", [P, KT, SEQ], F32R, a_m + 16 * KB)
        merged = sb("merged", [P, KT, SEQ], F32, a_m)
        hm_t = sb("hm_t", [P, KT, SEQ], F32, a_m + 16 * KB)
        tok = sb("tok", [P, 3, D], F32, a_m)
        qkv = sb("qkv", [P, NB, L], F32, a_head)
        at = a_head + NB * L * 4
        w_exp = sb("w_exp", [P, 640], F32, at)
        probs = sb("probs", [P, 640], F32, at + 2560)
        v_tok = sb("v_tok", [P, 3, HV + 1], F32, at + 5120)
        hm = sb("hm", [P, NT, HV], F32, at + 5120 + 3 * 257 * 4 + 20)
        t_cc = sb("t_cc", [P, NB, L], F32, a_tmp)
        t_z = sb("t_z", [P, NB, L], F32, a_tmp + NB * L * 4)
        t_y = sb("t_y", [P, NB, SEQ], F32, a_tmp + 2 * NB * L * 4)
        x32 = sb("x32", [P, 4, L], F32, a_tmp)
        gw = sb("gw", [P, KT, N_GATE], F32, a_tmp + NB * L * 4)
        sig = sb("sig", [P, NB, SEQ], F32, a_tmp)
        h1pre = sb("h1pre", [P, KT, SEQ], F32, a_y)
        xn1 = sb("xn1", [P, NT, D], F32, a_y + 16 * KB)
        h32 = sb("h32", [P, KT, SEQ], F32, a_y)
        hh1 = sb("hh1", [P, KT, SEQ], F32R, a_x)
        hl1 = sb("hl1", [P, KT, SEQ], F32R, a_x + KT * L * 4)
        h1 = sb("h1", [P, NT, D], F32, a_m)
        g1_bc = sb("g1_bc", [P, D], F32, a_m + 16 * KB)
        b1_bc = sb("b1_bc", [P, D], F32, a_m + 24 * KB)
        keys = sb("keys", [P, 2 * PH, P], F32, a_tmp + NB * SEQ * 4)
        keys_t = sb("keys_t", [P, 2 * PH, P], F32, a_head)
        qs = sb("qs", [P, NB, SEQ], F32, a_head + 8 * KB)
        sc_all = sb("sc_all", [P, NT, 2 * PH, NKEY], F32, a_y)
        u_rows = sb("u_rows", [P, RING, D], F32, a_stream)
        v_rows = sb("v_rows", [P, RING, D], F32, a_stream + 32 * KB)
        diag = sb("diag", [P, RING, P], F32, a_x)
        junk = sb("junk", [P, 2, D], BF16, a_x + 2 * KB)
        y2 = sb("y2", [P, NT, D], F32, a_x + 10 * KB)
        g2_bc = sb("g2_bc", [P, D], F32, a_y + 16 * KB)
        b2_bc = sb("b2_bc", [P, D], F32, a_y + 24 * KB)
        par_rows = sb("par_rows", [P, P], F32)
        bias_if = sb("bias_if", [HEADS, 2], F32)
        g1 = sb("g1", [HEADS, L], F32, a_head)
        g2 = sb("g2", [HEADS, L], F32, a_head + 2 * KB)
        cum_f = sb("cum_f", [HEADS, L], F32, a_head + 4 * KB)
        run_m = sb("run_m", [HEADS, L], F32, a_head + 6 * KB)
        a_tok = sb("a_tok", [P, 3, HEADS], F32)
        em_tok = sb("em_tok", [P, NT, HEADS], F32)
        st = sb("st", [P, 3, 4, 6], F32)
        mv = sb("mv", [P, 3, 2], F32)
        rstd = sb("rstd", [P, 3], F32)
        nmr = sb("nmr", [P, 3], F32)
        m_half = sb("m_half", [P, 4], F32)
        den = sb("den", [P, 2], F32)
        rden = sb("rden", [P, 2], F32)
        ssq = sb("ssq", [P, 2], F32)
        ssn = sb("ssn", [P, 2], F32)
        rrms = sb("rrms", [P, 2], F32)
        hscale = sb("hscale", [P, 2], F32)
        alpha_i = sb("alpha_i", [P, P], F32)
        zeros = sb("zeros", [P, P], F32)
        iota16 = sb("iota16", [P, TOPK], F32)
        a_top = area(8 * KB)
        sel = sb("sel", [HEADS, HEADS, P], F32, a_top)
        li = sb("li", [HEADS, L], F32, a_top + 4 * KB)
        fp = sb("fp", [HEADS, L], F32, a_top + 4 * KB + L * 4)
        ones_row = sb("ones_row", [HEADS, L], F32, a_top + 4 * KB + 2 * L * 4)
        sc = sb("sc", [P, 2, NKEY], F32, a_top)
        scw = sb("scw", [P, 2, NKEY], F32, a_top + 1 * KB)
        cand = sb("cand", [P, TOPK, TOPK], F32, a_top + 2 * KB)
        candw = sb("candw", [P, TOPK, TOPK], F32, a_top + 3 * KB)
        oh = sb("oh", [P, 2, TOPK, TOPK], F32, a_top + 4 * KB)
        ohv = sb("ohv", [P, 2, TOPK, TOPK], F32, a_top + 6 * KB)
        kv = sb("kv", [P, 2, TOPK], F32)
        ki = sb("ki", [P, 2, TOPK], U32)
        kif = sb("kif", [P, 2, TOPK], F32)
        best = sb("best", [P, TOPK], F32)
        pos = sb("pos", [P, TOPK], U32)
        pos2 = sb("pos2", [P, 2, TOPK], U32)
        pos2f = sb("pos2f", [P, 2, TOPK], F32)
        eid = sb("eid", [P, 2, TOPK], F32)
        eidx = sb("eidx", [P, TOPK], F32)
        nbest = sb("nbest", [P, 1], F32)
        pe_ = sb("pexp", [P, TOPK], F32)
        psm = sb("psum_exp", [P, 1], F32)
        prs = sb("prs", [P, 1], F32)
        idx_all = sb("idx_all", [P, NT * SLOTS], U32)
        g_all = sb("g_all", [P, NT * SLOTS], F32)
        idx_u = sb("idx_u", [P, 2, TOPK], U32)
        idx_v = sb("idx_v", [P, 2, TOPK], U32)
        dots = sb("dots", [P, 2, TOPK], F32)
        gel = sb("gel", [P, 2, TOPK], F32)
        coef = sb("coef", [P, 2, TOPK], F32)

        ps = ctx.enter_context(nc.psum_tensor("ps", [P, 8, 512], F32))

        sems = {}

        def S(name):
            if name not in sems:
                sems[name] = ctx.enter_context(nc.semaphore(name))
            return sems[name]

        for n in ("set_apart rows_cleared tok_in0 tok_in1 tok_in2 par_in bif_in gw_in keys_in bc1_in bc2_in out_done "
                  "raw_in0 raw_in1 raw_in2 raw_in3 hi_ready lo_ready halves_used block_done "
                  "blocks_evacuated const_ready ln0_stats ln0_rstd ln0_nmr ln0_norm x_transposed x32_ready "
                  "xh_ready x_split gate_w_used gates_done gates_read gate_exp gate_mid gate_log gate_rows "
                  "gate_bc gate_bc_read pool_chain dve_chain act_chain par_done par_read args_ready "
                  "weights_ready masked v_transposed scores_done v_copied probs_ready num_done "
                  "recip_ready ssq_ready rms_ready hm_done hm_transposed hmt_written cc_ready sig_ready "
                  "m32_ready hi_part y_ready merged_ready h1pre_ready h1_transposed ln1_stats ln1_rstd "
                  "ln1_nmr xn1_ready xn1_transposed h32_ready h1t_ready h1_ready keys_transposed "
                  "keys_copied qk_done sc_copied topk_neg topk_exp topk_done u_in0 u_in1 u_in2 u_in3 "
                  "v_in0 v_in1 v_in2 v_in3 dots_done rows_added diag_ready gelu_ready coef_ready "
                  "ffn_done ln2_stats ln2_rstd ln2_nmr xn2_ready y2_ready").split():
            S(n)
        def set_apart(eng):
            eng.sem_inc(S("set_apart"), 1)

        raw_in = [S(f"raw_in{j}") for j in range(CHUNKS)]
        u_in = [S(f"u_in{j}") for j in range(RING)]
        v_in = [S(f"v_in{j}") for j in range(RING)]

        block = ctx.enter_context(nc.Block())
        TOKR = [(0, META), (META, P), (META + P, P)]
        HCRED, BCRED = SLOT_N, NB

        @block.sync
        def _(sp):
            def load_group(G, sources):
                for j in range(CHUNKS):
                    if not (isinstance(G, int) and G == 0):
                        sp.wait_ge(S("lo_ready"), (G - 1) * HALVES + 2 * (j + 1))
                        set_apart(sp)
                    at = 0
                    for n, (w, c0, width) in enumerate(sources):
                        src = w[j * 4 * P:(j + 1) * 4 * P, bass.ds(c0, width)]
                        sp.dma_start(raw[:, j, :, at:at + width],
                                     src.rearrange("(k p) n -> p k n", p=P)).then_inc(raw_in[j], 16)
                        at += width

            sp.dma_start(tok[:META, 0, :], meta_tokens).then_inc(S("tok_in0"), 16)
            sp.dma_start(tok[:, 1, :], x[0, 0:P, :]).then_inc(S("tok_in1"), 16)
            sp.dma_start(tok[:, 2, :], x[0, P:2 * P, :]).then_inc(S("tok_in2"), 16)
            sp.wait_ge(S("rows_cleared"), 1)
            for n, v in enumerate((ln0_g, ln0_b, mh_norm_w[0], ln1_g[0], ln1_b[0])):
                sp.dma_start(par_rows[n * KT:(n + 1) * KT, :],
                             v.rearrange("(k p) -> k p", p=P)).then_inc(S("par_in"), 16)
            sp.dma_start(par_rows[CONV * KT:(CONV + CONV_W) * KT, :],
                         conv_w[0].rearrange("w (k p) -> (w k) p", p=P)).then_inc(S("par_in"), 16)
            for n in range(2):
                sp.dma_start(bias_if[:, n:n + 1], b_if[0, n * HEADS:(n + 1) * HEADS].rearrange("(h a) -> h a", a=1)
                             ).then_inc(S("bif_in"), 16)
            sp.dma_start(gw[:, :, :], w_in[:, C_GATE:C_GATE + N_GATE].rearrange("(k p) n -> p k n", p=P)
                         ).then_inc(S("gw_in"), 16)

            def head_sources(h):
                return [(w_in, C_Q + h * HQK, HQK), (w_in, C_K + h * HQK, HQK), (w_in, C_V + h * HV, HV)]

            load_group(0, head_sources(0))
            with sp.Fori(1, HEADS) as h:
                load_group(h, head_sources(h))
            with sp.Fori(0, 4) as g:
                for s, c in enumerate((C_CC, C_CX, C_CB)):
                    load_group(g * 3 + (G_CONV + s), [(w_in, g * GW + c, GW)])
            with sp.Fori(0, 4) as g:
                load_group(g * 2 + G_GA, [(w_in, g * GW + C_GA, GW)])
                load_group(g * 2 + (G_GA + 1), [(p_a, g * GW, GW)])
            with sp.Fori(0, 4) as g:
                load_group(g + G_O, [(w_in, g * GW + C_O, GW)])
            with sp.Fori(0, 4) as g:
                load_group(g * 2 + G_GB, [(w_in, g * GW + C_GB, GW)])
                load_group(g * 2 + (G_GB + 1), [(p_b, g * GW, GW)])
            with sp.Fori(0, 4) as g:
                load_group(g + G_WO, [(w_o, g * GW, GW)])
            with sp.Fori(0, 4) as g:
                load_group(g + G_WQ, [(peer_wq, g * GW, GW)])
            sp.wait_ge(S("h1_ready"), NT)
            sp.wait_ge(S("xn1_transposed"), 2 * NT)
            for t, v in ((g2_bc, ln2_g), (b2_bc, ln2_b)):
                sp.dma_start(t[:, :], v[0].partition_broadcast(P)).then_inc(S("bc2_in"), 16)
            for T in range(NT):
                sp.wait_ge(S("y2_ready"), T + 1)
                sp.dma_start(out[0, T * P:(T + 1) * P, :], y2[:, T, :]).then_inc(S("out_done"), 16)
            sp.wait_ge(S("out_done"), 16 * NT)

        @block.tensor
        def _(pe):
            def mm(o, a, b, start, stop):
                return nc.tensor.matmul(o, a, b, start=start, stop=stop)

            def group(G, rh, rl, cols, after=None):
                for hh in range(HALVES):
                    pe.wait_ge(S("hi_ready"), G * HALVES + (hh + 1))
                    pe.wait_ge(S("lo_ready"), G * HALVES + (hh + 1))
                    for nb in range(NB):
                        if hh == 0:
                            pe.wait_ge(S("blocks_evacuated"), G * NB + (nb + 1))
                        c0, c1 = cols(nb)
                        o = ps[:, nb, 0:c1 - c0]
                        for k2 in range(2):
                            kt = hh * 2 + k2
                            wh = hi[:, hh % SLOT_N, k2, nb * P:(nb + 1) * P]
                            wl = lo[:, hh % SLOT_N, k2, nb * P:(nb + 1) * P]
                            mm(o, wh, rh[:, kt, c0:c1], kt == 0, False)
                            mm(o, wh, rl[:, kt, c0:c1], False, False)
                            last = mm(o, wl, rh[:, kt, c0:c1], False, kt == KT - 1)
                        if nb == NB - 1:
                            last.then_inc(S("halves_used"), 1)
                        elif hh == HALVES - 1:
                            last.then_inc(S("block_done"), 1)
                    if after and hh in after:
                        after[hh]()

            full = lambda nb: (0, L)
            outs = lambda nb: (META, L)
            own = lambda nb: (0, SEQ)

            pe.sem_inc(S("halves_used"), HCRED)
            pe.sem_inc(S("blocks_evacuated"), BCRED)
            pe.sem_inc(S("hm_done"), 1)
            pe.sem_inc(S("hmt_written"), 2)

            pe.wait_ge(S("const_ready"), 1)
            pe.wait_ge(S("par_in"), 16 * 6)
            nc.tensor.transpose(ps[:, 0, 0:P], par_rows[:, :], ident[:, :]).then_inc(S("par_done"), 1)
            pe.wait_ge(S("ln0_norm"), 3)
            pe.wait_ge(S("gw_in"), 16)
            for kt in range(KT + 2):
                if kt < KT:
                    if kt >= 4:
                        pe.wait_ge(S("x32_ready"), kt - 3)
                    for n, (c0, cnt) in enumerate(TOKR):
                        last = nc.tensor.transpose(ps[:, 4 + kt % 4, c0:c0 + cnt], tok[:cnt, n, kt * P:(kt + 1) * P],
                                                   ident[:cnt, :cnt])
                    last.then_inc(S("x_transposed"), 1)
                k = kt - 2
                if k >= 0:
                    pe.wait_ge(S("x32_ready"), k + 1)
                    for n in range(2):
                        last = mm(ps[:HEADS, 2 + n, 0:L], gw[:, k, n * HEADS:(n + 1) * HEADS], x32[:, k % 4, :],
                                  k == 0, k == KT - 1)
                    last.then_inc(S("gate_w_used"), 1)

            def gate_rows():
                pe.wait_ge(S("gate_rows"), 1)
                for n, (c0, cnt) in enumerate(TOKR):
                    nc.tensor.transpose(ps[:cnt, 4, n * HEADS:(n + 1) * HEADS], g1[:, c0:c0 + cnt],
                                        ident[:HEADS, :HEADS])
                for T in range(NT):
                    c0, cnt = TOKR[T + 1]
                    last = nc.tensor.transpose(ps[:cnt, 4, (3 + T) * HEADS:(4 + T) * HEADS], g2[:, c0:c0 + cnt],
                                               ident[:HEADS, :HEADS])
                last.then_inc(S("gate_bc"), 1)
                for r in range(2):
                    if r:
                        pe.wait_ge(S("gate_bc_read"), 2)
                    for h in range(4 * r, 4 * r + 4):
                        last = mm(ps[:, 5 + (h % 4) // 2, (h % 2) * SEQ:(h % 2 + 1) * SEQ], sel[:, h, :],
                                  run_m[:, META:L], True, True)
                    last.then_inc(S("gate_bc"), 1)

            def mlstm_scores(h):
                pe.wait_ge(S("blocks_evacuated"), h * NB + NB + BCRED)
                pe.wait_ge(S("hm_done"), h + 1)
                pe.wait_ge(S("hmt_written"), h * 2 + 2)
                for vb in range(2):
                    for n, (c0, cnt) in enumerate(TOKR):
                        o = ps[:cnt, 5, vb * P:(vb + 1) * P] if n == 0 else \
                            ps[:, 4, (n - 1) * HV + vb * P:(n - 1) * HV + (vb + 1) * P]
                        last = nc.tensor.transpose(o, qkv[:, 2 + vb, c0:c0 + cnt], ident[:, :])
                last.then_inc(S("v_transposed"), 1)
                mm(ps[:, 6, 0:SEQ], qkv[:, 1, META:META + P], qkv[:, 0, META:L], True, True)
                mm(ps[:META, 6, SEQ:2 * SEQ], qkv[:, 1, 0:META], qkv[:, 0, META:L], True, True)
                mm(ps[:, 7, 0:P], qkv[:, 1, META + P:L], qkv[:, 0, META + P:L], True, True
                   ).then_inc(S("scores_done"), 1)

            def mlstm_values(h):
                pe.wait_ge(S("probs_ready"), h + 1)
                pe.wait_ge(S("v_copied"), h * 2 + 2)
                mm(ps[:, 4, 0:HV + 1], probs[:, 0:P], v_tok[:, 0, :], True, False)
                mm(ps[:, 4, 0:HV + 1], probs[:META, 384:512], v_tok[:META, 2, :], False, True)
                mm(ps[:, 5, 0:HV + 1], probs[:, 256:384], v_tok[:, 0, :], True, False)
                mm(ps[:, 5, 0:HV + 1], probs[:, 128:256], v_tok[:, 1, :], False, False)
                mm(ps[:, 5, 0:HV + 1], probs[:META, 512:640], v_tok[:META, 2, :], False, True
                   ).then_inc(S("num_done"), 1)

            def mlstm_transpose(h):
                pe.wait_ge(S("hm_done"), h + 2)
                for vb in range(2):
                    for T in range(NT):
                        last = nc.tensor.transpose(ps[:, 6, vb * SEQ + T * P:vb * SEQ + (T + 1) * P],
                                                   hm[:, T, vb * P:(vb + 1) * P], ident[:, :])
                last.then_inc(S("hm_transposed"), 1)

            def mlstm(h):
                return {0: lambda: mlstm_scores(h), 4: lambda: mlstm_values(h), 7: lambda: mlstm_transpose(h)}

            pe.wait_ge(S("x_split"), KT)
            pe.wait_ge(S("gates_read"), 2)
            head_cols = lambda nb: (META, L) if nb == 0 else (0, L)
            group(0, xh, xl, head_cols, {3: gate_rows})
            with pe.Fori(1, HEADS) as G:
                group(G, xh, xl, head_cols, mlstm(G - 1))
            group(G_CONV, xh, xl, full, mlstm(HEADS - 1))
            group(G_CONV + 1, xh, xl, full)
            group(G_CONV + 2, xh, xl, outs)
            with pe.Fori(1, 4) as g:
                group(g * 3 + G_CONV, xh, xl, full)
                group(g * 3 + (G_CONV + 1), xh, xl, full)
                group(g * 3 + (G_CONV + 2), xh, xl, outs)
            pe.wait_ge(S("y_ready"), 4)
            with pe.Fori(0, 4) as g:
                group(g * 2 + G_GA, xh, xl, outs)
                group(g * 2 + (G_GA + 1), yh, yl, own)
            with pe.Fori(0, 4) as g:
                group(g + G_O, xh, xl, outs)
            with pe.Fori(0, 4) as g:
                group(g * 2 + G_GB, xh, xl, outs)
                pe.wait_ge(S("y_ready"), 8)
                group(g * 2 + (G_GB + 1), yh, yl, own)
            pe.wait_ge(S("merged_ready"), 4)
            with pe.Fori(0, 4) as g:
                group(g + G_WO, mh, ml, own)

            pe.wait_ge(S("keys_in"), 16)
            for c in range(4):
                if c >= 2:
                    pe.wait_ge(S("keys_copied"), c - 1)
                for n in range(4):
                    last = nc.tensor.transpose(ps[:, 6 + c % 2, n * P:(n + 1) * P], keys[:, 4 * c + n, :], ident[:, :])
                last.then_inc(S("keys_transposed"), 1)
            pe.wait_ge(S("h1pre_ready"), KT)
            pe.wait_ge(S("keys_copied"), 4)
            for T in range(NT):
                for kt in range(KT):
                    last = nc.tensor.transpose(ps[:, 4 * T + kt // 4, (kt % 4) * P:(kt % 4 + 1) * P],
                                               h1pre[:, kt, T * P:(T + 1) * P], ident[:, :])
                last.then_inc(S("h1_transposed"), 1)
            for T in range(NT):
                pe.wait_ge(S("xn1_ready"), T + 1)
                for kt in range(KT):
                    last = nc.tensor.transpose(ps[:, 4 * T + kt // 4, (kt % 4) * P:(kt % 4 + 1) * P],
                                               xn1[:, T, kt * P:(kt + 1) * P], ident[:, :])
                last.then_inc(S("xn1_transposed"), 2)

            def router_scores(g):
                pe.wait_ge(S("blocks_evacuated"), (G_WQ + g) * NB + NB + BCRED)
                if g:
                    pe.wait_ge(S("sc_copied"), NT * g)
                for T in range(NT):
                    for nb in range(NB):
                        last = mm(ps[:, 4 + T, nb * NKEY:(nb + 1) * NKEY], qs[:, nb, T * P:(T + 1) * P],
                                  keys_t[:, g * NB + nb, :], True, True)
                    last.then_inc(S("qk_done"), 1)

            pe.wait_ge(S("h1t_ready"), 4)
            for g in range(4):
                group(G_WQ + g, hh1, hl1, own, {1: lambda: router_scores(g - 1)} if g else None)
            router_scores(3)

            def tile_open(T):
                pe.wait_ge(S("h1_ready"), T + 1)
                for q in range(4):
                    mm(ps[:, 4 * T + q, :], alpha_i[:, :], h1[:, T, q * 512:(q + 1) * 512], True, False)

            def add_rows(T, u):
                for k in range(TOPK):
                    pe.wait_ge(v_in[k % RING], u * 64 + 16 * (k // RING + 1))
                    pe.wait_ge(S("diag_ready"), u * TOPK + (k + 1))
                    for q in range(4):
                        last = mm(ps[:, 4 * T + q, :], diag[:, k % RING, :],
                                  v_rows[:, k % RING, q * 512:(q + 1) * 512], False, False)
                    last.then_inc(S("rows_added"), 1)

            def tile_close(T):
                for q in range(4):
                    last = mm(ps[:, 4 * T + q, :], zeros[:, :], h1[:, T, q * 512:(q + 1) * 512], False, True)
                last.then_inc(S("ffn_done"), 1)

            pe.sem_inc(S("rows_added"), RING)
            tile_open(0)
            with pe.Fori(0, 3) as i:
                add_rows(0, i * 2)
                add_rows(0, i * 2 + 1)
            add_rows(0, 6)
            add_rows(0, 7)
            tile_close(0)
            pe.wait_ge(S("sc_copied"), NT * 4)
            tile_open(1)
            with pe.Fori(4, 7) as i:
                add_rows(1, i * 2)
                add_rows(1, i * 2 + 1)
            add_rows(1, 14)
            add_rows(1, 15)
            tile_close(1)

        @block.scalar
        def _(act):
            chain = Steps(act, S("act_chain"))

            def A(o, i, f, **kw):
                return nc.scalar.activation(o, i, f, **kw)

            def split_hi(G, hh, head):
                act.wait_ge(raw_in[hh // 2], G * 48 + 48 if head else G * 16 + 16 * (2 * HEADS + 1))
                act.wait_ge(S("halves_used"), G * HALVES + (hh + 1))
                A(hi[:, hh % SLOT_N, :, :], raw[:, hh // 2, 2 * (hh % 2):2 * (hh % 2) + 2, :], ACT.Copy
                  ).then_inc(S("hi_ready"), 1)

            def halves(G, after=None, head=False, head_next=False, last=False):
                for n in range(AHEAD, HALVES if last else HALVES + AHEAD):
                    if n < HALVES:
                        split_hi(G, n, head)
                    else:
                        split_hi(G + 1, n - HALVES, head_next)
                    if after and n in after:
                        after[n]()
                if last:
                    for n in sorted(after or {}):
                        if n >= HALVES:
                            after[n]()

            def block_wait(G, nb):
                if nb < NB - 1:
                    act.wait_ge(S("block_done"), G * (NB - 1) + (nb + 1))
                else:
                    act.wait_ge(S("halves_used"), G * HALVES + HALVES + HCRED)

            def evacuate(G, dst, c0, f=ACT.Copy):
                for nb in range(NB):
                    block_wait(G, nb)
                    A(dst(nb), ps[:, nb, 0:c0], f).then_inc(S("blocks_evacuated"), 1)

            for n, cnt in enumerate((META, P, P)):
                act.wait_ge(S("ln0_nmr"), n + 1)
                A(tok[:cnt, n, :], tok[:cnt, n, :], ACT.Identity, scale=rstd[:cnt, n:n + 1],
                  bias=nmr[:cnt, n:n + 1]).then_inc(S("ln0_norm"), 1)
            act.wait_ge(S("par_read"), 1)
            for kt in range(KT):
                act.wait_ge(S("x_transposed"), kt + 1)
                if kt >= 4:
                    act.wait_ge(S("x_split"), kt - 3)
                    act.wait_ge(S("gate_w_used"), kt - 3)
                A(x32[:, kt % 4, :], ps[:, 4 + kt % 4, 0:L], ACT.Identity, scale=par[:, LN0G, kt:kt + 1],
                  bias=par[:, LN0B, kt:kt + 1]).then_inc(S("x32_ready"), 1)
            act.wait_ge(S("gate_w_used"), KT)
            act.wait_ge(S("bif_in"), 32)
            for n, t in enumerate((li, fp)):
                A(t[:, :], ps[:HEADS, 2 + n, 0:L], ACT.Identity, bias=bias_if[:, n:n + 1]).then_inc(S("gates_read"), 1)
            for hh in range(AHEAD):
                split_hi(0, hh, True)
            act.wait_ge(S("gate_mid"), 1)
            chain.link(A(g1[:, :], g1[:, :], ACT.Exp))
            A(g1[:, :], g1[:, :], ACT.Ln, bias=1.0).then_inc(S("gate_log"), 1)

            def gates_out():
                act.wait_ge(S("gate_bc"), 1)
                chain.link(A(a_tok[:META, 0, :], ps[:META, 4, 0:HEADS], ACT.Copy))
                chain.link(A(a_tok[:, 1:3, :], ps[:, 4, HEADS:3 * HEADS].rearrange("p (n h) -> p n h", n=2), ACT.Copy))
                A(em_tok[:, :, :], ps[:, 4, 3 * HEADS:5 * HEADS].rearrange("p (n h) -> p n h", n=2), ACT.Exp
                  ).then_inc(S("gate_bc_read"), 1)
                for r in range(2):
                    act.wait_ge(S("gate_bc"), 2 + r)
                    A(neg_m[:, 4 * r:4 * r + 4, :].rearrange("p (a b) t -> p a (b t)", a=2), ps[:, 5:7, :], ACT.Copy,
                      scale=-1.0).then_inc(S("gate_bc_read"), 1)

            def mlstm_copy_v(h):
                act.wait_ge(S("v_transposed"), h + 1)
                A(v_tok[:, 0:2, 0:HV], ps[:, 4, :].rearrange("p (n v) -> p n v", n=2), ACT.Copy).then_inc(S("v_copied"), 1)
                A(v_tok[:META, 2, 0:HV], ps[:META, 5, 0:HV], ACT.Copy).then_inc(S("v_copied"), 1)

            def mlstm_exp(h):
                act.wait_ge(S("args_ready"), h + 1)
                A(w_exp[:, 0:384], w_exp[:, 0:384], ACT.Exp)
                A(w_exp[:META, 384:640], w_exp[:META, 384:640], ACT.Exp).then_inc(S("weights_ready"), 1)

            def mlstm_square(h):
                act.wait_ge(S("recip_ready"), h + 1)
                for T in range(NT):
                    A(hm[:, T, :], ps[:, 4 + T, 0:HV], ACT.Square, scale=rden[:, T:T + 1],
                      accum_out=ssq[:, T:T + 1]).then_inc(S("ssq_ready"), 1)

            def mlstm_out(h):
                act.wait_ge(S("hm_transposed"), h + 1)
                for vb in range(2):
                    A(hm_t[:, bass.ds(h * 2 + vb, 1), :].rearrange("p a t -> p (a t)"),
                      ps[:, 6, vb * SEQ:(vb + 1) * SEQ], ACT.Copy).then_inc(S("hmt_written"), 1)

            def mlstm(h):
                return {4: lambda: mlstm_copy_v(h), 5: lambda: mlstm_exp(h), 9: lambda: mlstm_square(h)}

            to_qkv = lambda nb: qkv[:, nb, META:L] if nb == 0 else qkv[:, nb, :]

            def evacuate_head(G):
                for nb in range(NB):
                    block_wait(G, nb)
                    A(to_qkv(nb), ps[:, nb, 0:SEQ if nb == 0 else L], ACT.Copy).then_inc(S("blocks_evacuated"), 1)

            halves(0, {4: gates_out}, head=True, head_next=True)
            evacuate_head(0)
            with act.Fori(1, HEADS - 1) as G:
                halves(G, mlstm(G - 1), head=True, head_next=True)
                act.wait_ge(S("scores_done"), G)
                evacuate_head(G)
                mlstm_out(G - 1)
            G = HEADS - 1
            halves(G, mlstm(G - 1), head=True)
            act.wait_ge(S("scores_done"), G)
            evacuate_head(G)
            mlstm_out(G - 1)

            def conv_groups(g, after=None):
                G = g * 3 + G_CONV
                halves(G, after)
                evacuate(G, lambda nb: t_cc[:, nb, :], L)
                if after:
                    mlstm_out(HEADS - 1)
                halves(G + 1)
                halves(G + 2)
                act.wait_ge(S("m32_ready"), g + 1)
                A(yh[:, bass.ds(g * NB, NB), :], t_y[:, :, :], ACT.Copy).then_inc(S("hi_part"), 1)

            conv_groups(0, mlstm(HEADS - 1))
            with act.Fori(1, 4) as g:
                conv_groups(g)

            to_sig = lambda nb: sig[:, nb, :]
            with act.Fori(0, 4) as g:
                halves(g * 2 + G_GA)
                act.wait_ge(S("m32_ready"), g + 4)
                evacuate(g * 2 + G_GA, to_sig, SEQ, ACT.Sigmoid)
                halves(g * 2 + (G_GA + 1))
            with act.Fori(0, 4) as g:
                halves(g + G_O)
                act.wait_ge(S("m32_ready"), g + 8)
                evacuate(g + G_O, to_sig, SEQ, ACT.Sigmoid)
                act.wait_ge(S("m32_ready"), g + 9)
                A(yh[:, bass.ds(g * NB, NB), :], t_y[:, :, :], ACT.Copy).then_inc(S("hi_part"), 1)
            with act.Fori(0, 4) as g:
                halves(g * 2 + G_GB)
                act.wait_ge(S("m32_ready"), g + 12)
                evacuate(g * 2 + G_GB, to_sig, SEQ, ACT.Sigmoid)
                halves(g * 2 + (G_GB + 1))
                act.wait_ge(S("m32_ready"), g + 13)
                A(mh[:, bass.ds(g * NB, NB), :], t_y[:, :, :], ACT.Copy).then_inc(S("hi_part"), 1)
            with act.Fori(0, 4) as g:
                halves(g + G_WO)

            for c in range(4):
                act.wait_ge(S("keys_transposed"), c + 1)
                A(keys_t[:, 4 * c:4 * c + 4, :].rearrange("p a b -> p (a b)"), ps[:, 6 + c % 2, :], ACT.Copy
                  ).then_inc(S("keys_copied"), 1)
            for T in range(NT):
                act.wait_ge(S("ln1_nmr"), T + 1)
                A(xn1[:, T, :].rearrange("p (a b) -> p a b", a=4), ps[:, 4 * T:4 * T + 4, :], ACT.Identity,
                  scale=rstd[:, T:T + 1], bias=nmr[:, T:T + 1]).then_inc(S("xn1_ready"), 1)
            for T in range(NT):
                act.wait_ge(S("xn1_transposed"), 2 * (T + 1))
                for kt in range(KT):
                    A(h32[:, kt, T * P:(T + 1) * P], ps[:, 4 * T + kt // 4, (kt % 4) * P:(kt % 4 + 1) * P],
                      ACT.Identity, scale=par[:, LN1G, kt:kt + 1], bias=par[:, LN1B, kt:kt + 1]
                      ).then_inc(S("h32_ready"), 1)

            def copy_scores(g):
                for T in range(NT):
                    act.wait_ge(S("qk_done"), NT * g + T + 1)
                    A(sc_all[:, T, NB * g:NB * (g + 1), :].rearrange("p a b -> p (a b)"), ps[:, 4 + T, :], ACT.Copy
                      ).then_inc(S("sc_copied"), 1)

            def softmax_exp(u):
                act.wait_ge(S("topk_neg"), u + 1)
                A(pe_[:, :], best[:, :], ACT.Exp, bias=nbest[:, 0:1], accum_out=psm[:, 0:1]
                  ).then_inc(S("topk_exp"), 1)

            def router_work(g):
                return {6: lambda: copy_scores(g), 7: lambda: softmax_exp(2 * g), 9: lambda: softmax_exp(2 * g + 1)}

            act.wait_ge(S("h1t_ready"), 4)
            for g in range(4):
                halves(G_WQ + g, router_work(g - 1) if g else None, last=g == 3)
                if g == 3:
                    break
                if g:
                    act.wait_ge(S("qk_done"), NT * g)
                evacuate(G_WQ + g, lambda nb: qs[:, nb, :], SEQ)
            act.wait_ge(S("qk_done"), NT * 3)
            evacuate(G_WQ + 3, lambda nb: qs[:, nb, :], SEQ)
            copy_scores(3)
            softmax_exp(6)
            softmax_exp(7)

            def gelu(u, par_u):
                act.wait_ge(S("dots_done"), u * TOPK + (TOPK + RING))
                A(gel[:, par_u, :], dots[:, par_u, :], ACT.Gelu).then_inc(S("gelu_ready"), 1)

            def diagonals(u, par_u):
                act.wait_ge(S("coef_ready"), u + 1)
                for k in range(TOPK):
                    act.wait_ge(S("rows_added"), u * TOPK + (k + 1))
                    A(diag[:, k % RING, :], ident[:, :], ACT.Copy, scale=coef[:, par_u, k:k + 1]
                      ).then_inc(S("diag_ready"), 1)

            with act.Fori(0, 3) as i:
                for e in range(2):
                    u = i * 2 + (e + 1)
                    gelu(u - 1, e)
                    diagonals(u - 1, e)
                    softmax_exp(u + 7)
            for u in (7, 8):
                gelu(u - 1, (u - 1) % 2)
                diagonals(u - 1, (u - 1) % 2)
                softmax_exp(u + 7)

            def ln2(T):
                act.wait_ge(S("ln2_nmr"), T + 1)
                A(y2[:, T, :].rearrange("p (a b) -> p a b", a=4), ps[:, 4 * T:4 * T + 4, :], ACT.Identity,
                  scale=rstd[:, T:T + 1], bias=nmr[:, T:T + 1]).then_inc(S("xn2_ready"), 1)

            ln2(0)
            with act.Fori(4, 7) as i:
                for e in range(2):
                    u = i * 2 + (e + 1)
                    gelu(u - 1, e)
                    diagonals(u - 1, e)
            for u in (15, 16):
                gelu(u - 1, (u - 1) % 2)
                diagonals(u - 1, (u - 1) % 2)
            ln2(1)

        @block.vector
        def _(dve):
            chain = Steps(dve, S("dve_chain"))
            V = nc.vector

            def split_lo(G, hh):
                dve.wait_ge(S("hi_ready"), G * HALVES + (hh + 1))
                V.tensor_tensor(lo[:, hh % SLOT_N, :, :], raw[:, hh // 2, 2 * (hh % 2):2 * (hh % 2) + 2, :],
                                hi[:, hh % SLOT_N, :, :].bitcast(F32), ALU.subtract).then_inc(S("lo_ready"), 1)

            def halves(G, after=None, last=False):
                for n in range(AHEAD, HALVES if last else HALVES + AHEAD):
                    split_lo(*((G, n) if n < HALVES else (G + 1, n - HALVES)))
                    if after and n in after:
                        after[n]()
                if last:
                    for n in sorted(after or {}):
                        if n >= HALVES:
                            after[n]()

            def block_wait(G, nb):
                if nb < NB - 1:
                    dve.wait_ge(S("block_done"), G * (NB - 1) + (nb + 1))
                else:
                    dve.wait_ge(S("halves_used"), G * HALVES + HALVES + HCRED)

            def blk(t, g, nb):
                return t[:, bass.ds(g * NB + nb, 1), :].rearrange("p a t -> p (a t)")

            def res(t, g, nb):
                return t[:, bass.ds(g * NB + nb, 1), META:L].rearrange("p a t -> p (a t)").bitcast(F32)

            def stats(src, n, cnt, done):
                for q in range(4):
                    ins = V.bn_stats(st[:cnt, n, q, :], src(q))
                chain.link(ins)
                chain.link(V.bn_aggr(mv[:cnt, n, :], st[:cnt, n, :, :].rearrange("p a b -> p (a b)")))
                V.tensor_scalar(rstd[:cnt, n:n + 1], mv[:cnt, n, 1:2], EPS, None, ALU.add).then_inc(S(done), 1)

            def neg_mean(n, cnt, done):
                V.scalar_tensor_tensor(nmr[:cnt, n:n + 1], mv[:cnt, n, 0:1], -1.0, rstd[:cnt, n:n + 1],
                                       ALU.mult, ALU.mult).then_inc(S(done), 1)

            V.memset(ones_row[:, :], 1.0)
            V.memset(par_rows[:, :], 0.0).then_inc(S("rows_cleared"), 1)
            for n, cnt in enumerate((META, P, P)):
                dve.wait_ge(S(f"tok_in{n}"), 16)
                stats(lambda q: tok[:cnt, n, q * 512:(q + 1) * 512], n, cnt, "ln0_stats")
            for n, cnt in enumerate((META, P, P)):
                dve.wait_ge(S("ln0_rstd"), n + 1)
                neg_mean(n, cnt, "ln0_nmr")
            dve.wait_ge(S("par_done"), 1)
            V.tensor_copy(par[:, :, :].rearrange("p a b -> p (a b)"), ps[:, 0, 0:P]).then_inc(S("par_read"), 1)
            V.memset(v_tok[:, :, HV:HV + 1], 1.0)
            for kt in range(KT):
                dve.wait_ge(S("x32_ready"), kt + 1)
                chain.link(V.tensor_copy(xh[:, kt, :], x32[:, kt % 4, :]))
                V.tensor_tensor(xl[:, kt, :], x32[:, kt % 4, :], xh[:, kt, :].bitcast(F32), ALU.subtract
                                ).then_inc(S("x_split"), 1)
            for hh in range(AHEAD):
                split_lo(0, hh)
            dve.wait_ge(S("gates_read"), 2)
            V.scalar_tensor_tensor(g1[:, :], fp[:, :], -1.0, fp[:, :], ALU.mult, ALU.min).then_inc(S("gate_mid"), 1)
            chain.link(V.tensor_scalar(g2[:, :], fp[:, :], 0.0, None, ALU.min))
            dve.wait_ge(S("gate_log"), 1)
            chain.link(V.tensor_tensor(g2[:, :], g2[:, :], g1[:, :], ALU.subtract))
            chain.link(V.tensor_tensor_scan(cum_f[:, :], ones_row[:, :], g2[:, :], 0.0, ALU.mult, ALU.add))
            chain.link(V.tensor_tensor(g1[:, :], li[:, :], cum_f[:, :], ALU.subtract))
            chain.link(V.tensor_tensor_scan(run_m[:, :], g1[:, :], g1[:, :], 0.0, ALU.max, ALU.max))
            V.scalar_tensor_tensor(g2[:, :], cum_f[:, :], -1.0, run_m[:, :], ALU.mult, ALU.subtract
                                   ).then_inc(S("gate_rows"), 1)

            two = lambda ap: ap.rearrange("p (a b) -> p a b", b=P)
            w_diag0 = lambda t: t[:, 0:512].rearrange("p (a b) -> p a b", b=256)[:, :, 0:P]

            def hrow(t, h, c0, c1, cnt=P):
                return t[:cnt, bass.ds(h, 1), c0:c1].rearrange("p a t -> p (a t)")

            def acol(n, h, cnt=P):
                return a_tok[:cnt, n, bass.ds(h, 1)]

            def mlstm_args(h):
                V.tensor_scalar(w_diag0(w_exp), two(hrow(neg_m, h, 0, SEQ)), acol(1, h), 0.0, ALU.add, ALU.min)
                V.tensor_scalar(w_exp[:, P:2 * P], hrow(neg_m, h, P, SEQ), acol(2, h), 0.0, ALU.add, ALU.min)
                V.tensor_scalar(w_exp[:META, 384:640], hrow(neg_m, h, 0, SEQ, META), acol(0, h, META), 0.0,
                                ALU.add, ALU.min).then_inc(S("args_ready"), 1)

            def mlstm_probs(h):
                dve.wait_ge(S("scores_done"), h + 1)
                dve.wait_ge(S("masked"), h + 1)
                V.scalar_tensor_tensor(w_diag0(probs), two(ps[:, 6, 0:SEQ]), QSCALE, w_diag0(w_exp), ALU.mult, ALU.mult)
                V.scalar_tensor_tensor(probs[:, P:2 * P], ps[:, 7, 0:P], QSCALE, w_exp[:, P:2 * P], ALU.mult, ALU.mult)
                V.scalar_tensor_tensor(probs[:META, 384:640], ps[:META, 6, SEQ:2 * SEQ], QSCALE,
                                       w_exp[:META, 384:640], ALU.mult, ALU.mult).then_inc(S("probs_ready"), 1)

            def mlstm_den(h):
                dve.wait_ge(S("num_done"), h + 1)
                for T in range(NT):
                    ins = V.tensor_scalar(den[:, T:T + 1], ps[:, 4 + T, HV:HV + 1], -1.0, em_tok[:, T, bass.ds(h, 1)],
                                          ALU.mult, ALU.max)
                chain.link(ins)
                for T in range(NT):
                    ins = V.scalar_tensor_tensor(den[:, T:T + 1], ps[:, 4 + T, HV:HV + 1], 1.0, den[:, T:T + 1],
                                                 ALU.mult, ALU.max)
                chain.link(ins)
                V.reciprocal(rden[:, :], den[:, :]).then_inc(S("recip_ready"), 1)

            def mlstm_norm(h):
                dve.wait_ge(S("rms_ready"), h + 1)
                chain.link(V.tensor_tensor(hscale[:, :], rden[:, :], rrms[:, :], ALU.mult))
                V.tensor_scalar(hm[:, 0, :], ps[:, 4, 0:HV], hscale[:, 0:1], None, ALU.mult)
                V.tensor_scalar(hm[:, 1, :], ps[:, 5, 0:HV], hscale[:, 1:2], None, ALU.mult).then_inc(S("hm_done"), 1)

            def mlstm(h):
                return {4: lambda: mlstm_args(h), 6: lambda: mlstm_probs(h), 8: lambda: mlstm_den(h),
                        10: lambda: mlstm_norm(h)}

            halves(0)
            dve.wait_ge(S("gate_bc_read"), 3)
            with dve.Fori(1, HEADS) as G:
                chain.loop(G - 1, 3)
                halves(G, mlstm(G - 1))
                chain.end(HEADS - 1)

            def conv_groups(g, after=None):
                G = g * 3 + G_CONV
                halves(G, after)
                halves(G + 1)
                for nb in range(NB):
                    block_wait(G + 1, nb)
                    ins = V.tensor_tensor(t_z[:, nb, :], ps[:, nb, 0:L], t_cc[:, nb, :], ALU.mult)
                    ins.then_inc(S("blocks_evacuated"), 1)
                w = lambda k, nb: par[:, CONV + k, bass.ds(g * NB + nb, 1)]
                dve.wait_ge(S("blocks_evacuated"), G * NB + (2 * NB + BCRED))
                for nb in range(NB):
                    ins = V.tensor_scalar(t_y[:, nb, :], t_z[:, nb, META - 2:L - 2], w(0, nb), None, ALU.mult)
                chain.link(ins)
                for k in (1, 2):
                    for nb in range(NB):
                        ins = V.scalar_tensor_tensor(t_y[:, nb, :], t_z[:, nb, META - 2 + k:L - 2 + k], w(k, nb),
                                                     t_y[:, nb, :], ALU.mult, ALU.add)
                    chain.link(ins)
                halves(G + 2)
                for nb in range(NB):
                    block_wait(G + 2, nb)
                    V.tensor_tensor(t_y[:, nb, :], ps[:, nb, 0:SEQ], t_y[:, nb, :], ALU.mult
                                    ).then_inc(S("blocks_evacuated"), 1)
                dve.wait_ge(S("blocks_evacuated"), G * NB + (3 * NB + BCRED))
                dve.sem_inc(S("m32_ready"), 1)
                dve.wait_ge(S("hi_part"), g + 1)
                V.tensor_tensor(yl[:, bass.ds(g * NB, NB), :], t_y[:, :, :], yh[:, bass.ds(g * NB, NB), :].bitcast(F32),
                                ALU.subtract).then_inc(S("y_ready"), 1)

            conv_groups(0, mlstm(HEADS - 1))
            with dve.Fori(1, 4) as g:
                chain.loop(g - 1, 3)
                conv_groups(g)
                chain.end(3)

            with dve.Fori(0, 4) as g:
                halves(g * 2 + G_GA)
                halves(g * 2 + (G_GA + 1))
                for nb in range(NB):
                    block_wait(g * 2 + (G_GA + 1), nb)
                    V.tensor_tensor(blk(merged, g, nb), ps[:, nb, 0:SEQ], sig[:, nb, :], ALU.mult
                                    ).then_inc(S("blocks_evacuated"), 1)
                dve.wait_ge(S("blocks_evacuated"), g * 2 * NB + ((G_GA + 2) * NB + BCRED))
                dve.sem_inc(S("m32_ready"), 1)
            with dve.Fori(0, 4) as g:
                halves(g + G_O)
                chain.loop(g, 1)
                dve.wait_ge(S("blocks_evacuated"), g * NB + ((G_O + 1) * NB + BCRED))
                for nb in range(NB):
                    ins = V.scalar_tensor_tensor(t_y[:, nb, :], sig[:, nb, :], par[:, MHW, bass.ds(g * NB + nb, 1)],
                                                 blk(hm_t, g, nb), ALU.mult, ALU.mult)
                chain.link(ins)
                dve.sem_inc(S("m32_ready"), 1)
                dve.wait_ge(S("hi_part"), g + 5)
                V.tensor_tensor(yl[:, bass.ds(g * NB, NB), :], t_y[:, :, :], yh[:, bass.ds(g * NB, NB), :].bitcast(F32),
                                ALU.subtract).then_inc(S("y_ready"), 1)
                chain.end(4)
            with dve.Fori(0, 4) as g:
                halves(g * 2 + G_GB)
                halves(g * 2 + (G_GB + 1))
                chain.loop(g, 1)
                for nb in range(NB):
                    block_wait(g * 2 + (G_GB + 1), nb)
                    V.tensor_tensor(t_y[:, nb, :], ps[:, nb, 0:SEQ], sig[:, nb, :], ALU.mult
                                    ).then_inc(S("blocks_evacuated"), 1)
                dve.wait_ge(S("blocks_evacuated"), g * 2 * NB + ((G_GB + 2) * NB + BCRED))
                chain.link(V.tensor_tensor(t_y[:, :, :], t_y[:, :, :], merged[:, bass.ds(g * NB, NB), :], ALU.add))
                dve.sem_inc(S("m32_ready"), 1)
                dve.wait_ge(S("hi_part"), g + 9)
                V.tensor_tensor(ml[:, bass.ds(g * NB, NB), :], t_y[:, :, :], mh[:, bass.ds(g * NB, NB), :].bitcast(F32),
                                ALU.subtract).then_inc(S("merged_ready"), 1)
                chain.end(4)
            with dve.Fori(0, 4) as g:
                halves(g + G_WO)
                chain.loop(g, 1)
                for nb in range(NB):
                    block_wait(g + G_WO, nb)
                    ins = V.scalar_tensor_tensor(blk(h1pre, g, nb), res(xh, g, nb), ALPHA, ps[:, nb, 0:SEQ],
                                                 ALU.mult, ALU.add)
                    ins.then_inc(S("blocks_evacuated"), 1)
                dve.wait_ge(S("blocks_evacuated"), g * NB + ((G_WO + 1) * NB + BCRED))
                chain.link(V.memset(nbest[:, :], 0.0))
                for nb in range(NB):
                    V.scalar_tensor_tensor(blk(h1pre, g, nb), res(xl, g, nb), ALPHA, blk(h1pre, g, nb),
                                           ALU.mult, ALU.add).then_inc(S("h1pre_ready"), 1)
                chain.end(4)

            for T in range(NT):
                dve.wait_ge(S("h1_transposed"), T + 1)
                stats(lambda q: ps[:, 4 * T + q, :], T, P, "ln1_stats")
            for T in range(NT):
                dve.wait_ge(S("ln1_rstd"), T + 1)
                neg_mean(T, P, "ln1_nmr")
            for c in range(4):
                dve.wait_ge(S("h32_ready"), KT + 4 * (c + 1))
                chain.link(V.tensor_copy(hh1[:, 4 * c:4 * c + 4, :], h32[:, 4 * c:4 * c + 4, :]))
                V.tensor_tensor(hl1[:, 4 * c:4 * c + 4, :], h32[:, 4 * c:4 * c + 4, :],
                                hh1[:, 4 * c:4 * c + 4, :].bitcast(F32), ALU.subtract).then_inc(S("h1t_ready"), 1)

            def topk(u, scores):
                def step(ins):
                    chain.link(ins)
                    set_apart(dve)

                step(V.tensor_copy(sc[:, :, :], scores))
                for p in range(2):
                    ins = V.max(kv[:, p, 0:8], sc[:, p, :])
                step(ins)
                for p in range(2):
                    V.max_index(ki[:, p, 0:8], kv[:, p, 0:8], sc[:, p, :])
                    ins = V.match_replace(scw[:, p, :], kv[:, p, 0:8], sc[:, p, :], NEG)
                step(ins)
                for p in range(2):
                    ins = V.max(kv[:, p, 8:16], scw[:, p, :])
                step(ins)
                for p in range(2):
                    ins = V.max_index(ki[:, p, 8:16], kv[:, p, 8:16], scw[:, p, :])
                step(ins)
                V.tensor_copy(kif[:, :, :], ki[:, :, :])
                step(V.tensor_tensor(cand[:, :, :], kv[:, 0, :].unsqueeze(2).to_broadcast([P, TOPK, TOPK]),
                                           kv[:, 1, :].unsqueeze(1).to_broadcast([P, TOPK, TOPK]), ALU.add))
                flat = lambda t: t[:, :, :].rearrange("p a b -> p (a b)")
                step(V.max(best[:, 0:8], flat(cand)))
                V.max_index(pos[:, 0:8], best[:, 0:8], flat(cand))
                step(V.match_replace(flat(candw), best[:, 0:8], flat(cand), NEG))
                step(V.max(best[:, 8:16], flat(candw)))
                step(V.max_index(pos[:, 8:16], best[:, 8:16], flat(candw)))
                V.tensor_scalar(nbest[:, :], best[:, 0:1], -1.0, None, ALU.mult).then_inc(S("topk_neg"), 1)
                V.tensor_scalar(pos2[:, 0, :], pos[:, :], 4, None, ALU.logical_shift_right)
                step(V.tensor_scalar(pos2[:, 1, :], pos[:, :], TOPK - 1, None, ALU.bitwise_and))
                step(V.tensor_copy(pos2f[:, :, :], pos2[:, :, :]))
                for p in range(2):
                    ins = V.tensor_tensor(oh[:, p, :, :], pos2f[:, p, :].unsqueeze(2).to_broadcast([P, TOPK, TOPK]),
                                          iota16[:, :].unsqueeze(1).to_broadcast([P, TOPK, TOPK]), ALU.is_equal)
                step(ins)
                for p in range(2):
                    ins = V.tensor_tensor(ohv[:, p, :, :], oh[:, p, :, :],
                                          kif[:, p, :].unsqueeze(1).to_broadcast([P, TOPK, TOPK]), ALU.mult)
                step(ins)
                step(V.tensor_reduce(eid[:, :, :], ohv[:, :, :, :], AX.X, ALU.add))
                step(V.scalar_tensor_tensor(eidx[:, :], eid[:, 0, :], float(NKEY), eid[:, 1, :], ALU.mult, ALU.add))
                step(V.tensor_copy(idx_all[:, bass.ds(u * TOPK, TOPK)], eidx[:, :]))
                dve.wait_ge(S("topk_exp"), u + 1)
                step(V.reciprocal(prs[:, :], psm[:, :]))
                V.tensor_scalar(g_all[:, bass.ds(u * TOPK, TOPK)], pe_[:, :], prs[:, 0:1], None, ALU.mult
                                ).then_inc(S("topk_done"), 1)

            TOPK_LINKS = 18

            def scores_of(T, h):
                return sc_all[:, T, bass.ds(h * 2, 2), :]

            def router_work(g):
                def work(e):
                    def f():
                        if e == 0:
                            dve.wait_ge(S("sc_copied"), NT * (g + 1))
                        topk(2 * g + e, scores_of(0, 2 * g + e))
                    return f
                return {6: work(0), 8: work(1)}

            dve.wait_ge(S("const_ready"), 1)
            for g in range(4):
                halves(G_WQ + g, router_work(g - 1) if g else None, last=g == 3)
            w = router_work(3)
            w[6]()
            w[8]()

            dve.sem_inc(S("dots_done"), RING)

            def dot(T, u, par_u, k):
                dve.wait_ge(u_in[k % RING], u * 64 + 16 * (k // RING + 1))
                dve.wait_ge(S("dots_done"), u * TOPK + (k + RING - 1))
                V.scalar_tensor_tensor(junk[:, k % 2, :], u_rows[:, k % RING, :], 1.0, h1[:, T, :], ALU.mult, ALU.mult,
                                       accum_out=dots[:, par_u, k:k + 1]).then_inc(S("dots_done"), 1)

            def coefs(u, par_u):
                dve.wait_ge(S("gelu_ready"), u + 1)
                V.tensor_tensor(coef[:, par_u, :], gel[:, par_u, :], g_all[:, bass.ds(u * TOPK, TOPK)], ALU.mult
                                ).then_inc(S("coef_ready"), 1)

            def unit(T, u, par_u):
                for k in range(TOPK):
                    dot(T, u, par_u, k)
                    if k == 0:
                        coefs(u - 1, 1 - par_u)

            dve.wait_ge(S("h1_ready"), 1)
            for k in range(TOPK):
                dot(0, 0, 0, k)
            with dve.Fori(0, 3) as i:
                chain.loop(i, 2 * TOPK_LINKS)
                for e in range(2):
                    unit(0, i * 2 + (e + 1), 1 - e)
                    topk(i * 2 + (e + 8), scores_of(1, i * 2 + e))
                chain.end(3)
            unit(0, 7, 1)
            topk(14, scores_of(1, 6))
            dve.wait_ge(S("h1_ready"), 2)
            unit(1, 8, 0)
            topk(15, scores_of(1, 7))

            def ln2(T):
                dve.wait_ge(S("ffn_done"), T + 1)
                stats(lambda q: ps[:, 4 * T + q, :], T, P, "ln2_stats")
                dve.wait_ge(S("ln2_rstd"), T + 1)
                neg_mean(T, P, "ln2_nmr")
                dve.wait_ge(S("bc2_in"), 32)
                dve.wait_ge(S("xn2_ready"), T + 1)
                chain.link(V.tensor_tensor(y2[:, T, :], y2[:, T, :], g2_bc[:, :], ALU.mult))
                V.tensor_tensor(y2[:, T, :], y2[:, T, :], b2_bc[:, :], ALU.add).then_inc(S("y2_ready"), 1)

            ln2(0)
            with dve.Fori(4, 7) as i:
                for e in range(2):
                    unit(1, i * 2 + (e + 1), 1 - e)
            unit(1, 15, 1)
            coefs(15, 1)
            ln2(1)

        @block.gpsimd
        def _(pool):
            chain = Steps(pool, S("pool_chain"))
            Q = nc.gpsimd
            chain.link(Q.memset(ident[:, :], 0.0))
            chain.link(Q.affine_select(out=ident[:, :], in_=ident[:, :], compare_op=ALU.not_equal, fill=1.0, base=0,
                                       pattern=[[-1, P]], channel_multiplier=1))
            chain.link(Q.memset(alpha_i[:, :], 0.0))
            chain.link(Q.affine_select(out=alpha_i[:, :], in_=alpha_i[:, :], compare_op=ALU.not_equal, fill=ALPHA,
                                       base=0, pattern=[[-1, P]], channel_multiplier=1))
            chain.link(Q.memset(sel[:, :, :], 0.0))
            chain.link(Q.affine_select(out=sel[:, :, :], in_=sel[:, :, :], compare_op=ALU.not_equal, fill=1.0, base=0,
                                       pattern=[[-1, HEADS], [0, P]], channel_multiplier=1))
            chain.link(Q.memset(zeros[:, :], 0.0))
            chain.link(Q.memset(m_half[:, :], -0.5))
            Q.iota(iota16[:, :], [[1, TOPK]], base=0, channel_multiplier=0, allow_small_or_imprecise_dtypes=True
                   ).then_inc(S("const_ready"), 1)

            def rsqrt(name, n, cnt, count):
                pool.wait_ge(S(name + "_stats"), count)
                Q.tensor_tensor(rstd[:cnt, n:n + 1], rstd[:cnt, n:n + 1], m_half[:cnt, 0:1], ALU.pow
                                ).then_inc(S(name + "_rstd"), 1)

            for n, cnt in enumerate((META, P, P)):
                rsqrt("ln0", n, cnt, n + 1)

            def mlstm(h):
                pool.wait_ge(S("weights_ready"), h + 1)
                set_apart(pool)
                blocks = w_exp[:, 0:2 * P].rearrange("p (a b) -> p a b", b=P)
                Q.affine_select(out=blocks, in_=blocks, compare_op=ALU.is_ge, fill=0.0, base=0,
                                pattern=[[0, 2], [1, P]], channel_multiplier=-1).then_inc(S("masked"), 1)
                pool.wait_ge(S("ssq_ready"), h * 2 + 2)
                set_apart(pool)
                chain.link(Q.tensor_scalar(ssn[:, :], ssq[:, :], 1.0 / HV, EPS, ALU.mult, ALU.add))
                Q.tensor_tensor(rrms[:, :], ssn[:, :], m_half[:, 0:2], ALU.pow).then_inc(S("rms_ready"), 1)

            with pool.Fori(0, HEADS) as h:
                chain.loop(h, 1)
                mlstm(h)
                chain.end(HEADS)

            pool.wait_ge(S("merged_ready"), 4)
            pool.dma_start(keys[:, :, :], keys_rows).then_inc(S("keys_in"), 16)
            pool.wait_ge(S("h1pre_ready"), KT)
            for t, v in ((g1_bc, ln1_g), (b1_bc, ln1_b)):
                pool.dma_start(t[:, :], v[0].partition_broadcast(P)).then_inc(S("bc1_in"), 16)
            for T in range(NT):
                rsqrt("ln1", T, P, T + 1)
            pool.wait_ge(S("bc1_in"), 32)
            for T in range(NT):
                pool.wait_ge(S("xn1_ready"), T + 1)
                chain.link(Q.tensor_tensor(h1[:, T, :], xn1[:, T, :], g1_bc[:, :], ALU.mult))
                Q.tensor_tensor(h1[:, T, :], h1[:, T, :], b1_bc[:, :], ALU.add).then_inc(S("h1_ready"), 1)

            def stage(dst, u, par_u):
                pool.wait_ge(S("topk_done"), u + 1)
                set_apart(pool)
                chain.link(Q.tensor_copy(dst[:, par_u, :], idx_all[:, bass.ds(u * TOPK, TOPK)]))

            def gather_u(u, par_u, k):
                pool.wait_ge(S("dots_done"), u * TOPK + (k + 1))
                set_apart(pool)
                Q.indirect_dma_start(u_rows[:, k % RING, :], None, peer_u,
                                     bass.IndirectOffsetOnAxis(ap=idx_u[:, par_u, k:k + 1], axis=0)
                                     ).then_inc(u_in[k % RING], 16)

            def gather_v(u, par_u, k):
                pool.wait_ge(S("rows_added"), u * TOPK + (k + 1))
                set_apart(pool)
                Q.indirect_dma_start(v_rows[:, k % RING, :], None, peer_v,
                                     bass.IndirectOffsetOnAxis(ap=idx_v[:, par_u, k:k + 1], axis=0)
                                     ).then_inc(v_in[k % RING], 16)

            def unit(u, par_u):
                for k in range(TOPK):
                    if k == TOPK // 2:
                        if not isinstance(u, int) or u < 15:
                            stage(idx_u, u + 1, 1 - par_u)
                            set_apart(pool)
                        stage(idx_v, u, par_u)
                    gather_u(u, par_u, k)
                    gather_v(u - 1, 1 - par_u, k)

            pool.wait_ge(S("halves_used"), GROUPS * HALVES + HCRED)
            stage(idx_u, 0, 0)
            for k in range(TOPK):
                gather_u(0, 0, k)
            stage(idx_u, 1, 1)
            stage(idx_v, 0, 0)
            with pool.Fori(0, 3) as i:
                chain.loop(i, 4)
                for e in range(2):
                    unit(i * 2 + (e + 1), 1 - e)
                chain.end(3)
            unit(7, 1)
            unit(8, 0)
            rsqrt("ln2", 0, P, 1)
            with pool.Fori(4, 7) as i:
                chain.loop(i - 4, 4)
                for e in range(2):
                    unit(i * 2 + (e + 1), 1 - e)
                chain.end(3)
            unit(15, 1)
            for k in range(TOPK):
                gather_v(15, 1, k)
            rsqrt("ln2", 1, P, 2)


_INS = ["x", "meta_tokens", "ln0_g", "ln0_b", "w_in", "b_if", "conv_w", "mh_norm_w", "p_a", "p_b", "w_o",
        "ln1_g", "ln1_b", "peer_wq", "peer_keys", "peer_u", "peer_v", "ln2_g", "ln2_b"]


def kernel(**inputs):
    import numpy as _np
    import concourse.bacc as _bacc
    from concourse import mybir as _mybir
    from concourse.bass_utils import run_bass_kernel_spmd as _run

    nc = _bacc.Bacc("TRN2", target_bir_lowering=False, num_devices=1)
    arrays, args = {}, []
    for name in _INS:
        a = _np.ascontiguousarray(inputs[name])
        arrays[f"in_{name}"] = a
        args.append(nc.dram_tensor(f"in_{name}", a.shape, _mybir.dt.from_np(a.dtype), kind="ExternalInput").ap())
    args.append(nc.dram_tensor("out_0", (1, SEQ, D), F32, kind="ExternalOutput").ap())
    decoder_layer(nc, *args)
    r = _run(nc, [arrays], core_ids=[0])
    return r.results[0]["out_0"]
```

```python
from contextlib import ExitStack

import numpy as np
import concourse.bass as bass
from concourse import mybir

F32 = mybir.dt.float32
F32R = mybir.dt.float32r
BF16 = mybir.dt.bfloat16
U32 = mybir.dt.uint32
ALU = mybir.AluOpType
ACT = mybir.ActivationFunctionType
AX = mybir.AxisListType

P = 128
D = 2048
KT = D // P
SEQ, META = 256, 16
L = SEQ + META
NT = SEQ // P
HEADS, HQK, HV = 8, 128, 256
CONV_W = 3
N_GATE = 2 * HEADS
PH, NKEY, TOPK = 8, 128, 16
SLOTS = PH * TOPK
ALPHA = 2 ** 0.25
EPS = 1e-5
QSCALE = HQK ** -0.5
NEG = -3.0e38

C_CB, C_CC, C_CX = 0, D, 2 * D
C_Q = 3 * D
C_K = C_Q + HEADS * HQK
C_V = C_K + HEADS * HQK
C_O = C_V + D
C_GATE = C_O + D
C_GA = C_GATE + N_GATE
C_GB = C_GA + D

NB = 4
GW = NB * P
CHUNKS, HALVES = 4, 8
SLOT_N = 4
FIRST_SPLITS = (2, 4, 6, 8, 10, 12, 14)
TAIL_Q = 2
AHEAD = 3
G_CONV, G_GA, G_O, G_GB, G_WO, G_WQ = 8, 20, 28, 32, 40, 44
GROUPS = 48

QN = 2
QW = D // QN
RING = 4


class Steps:

    def __init__(self, eng, sem):
        self.eng, self.sem, self.base, self.k, self.i, self.per = eng, sem, 0, 0, None, 0

    def loop(self, i, per):
        self.base, self.k, self.i, self.per = self.base + self.k, 0, i, per

    def end(self, n):
        assert self.k == self.per, (self.k, self.per)
        self.base, self.k, self.i = self.base + n * self.per, 0, None

    def link(self, ins):
        ins.then_inc(self.sem, 1)
        self.k += 1
        at = self.base + self.k
        self.eng.wait_ge(self.sem, at if self.i is None else self.i * self.per + at)


def decoder_layer(nc, x, meta_tokens, ln0_g, ln0_b, w_in, b_if, conv_w, mh_norm_w, p_a, p_b, w_o,
                  ln1_g, ln1_b, peer_wq, peer_keys, peer_u, peer_v, ln2_g, ln2_b, out):
    w_in, p_a, p_b, w_o, peer_wq = w_in[0], p_a[0], p_b[0], w_o[0], peer_wq[0]
    peer_u, peer_v = peer_u[0], peer_v[0]
    keys_rows = peer_keys[0].rearrange("h p n k -> n (h p) k")

    ctx = ExitStack()
    with ctx:
        GF = 32
        GCOLS = GF + HEADS

        top = [-(-nc.sbuf_base // 64) * 64]

        def area(nbytes):
            at = top[0]
            top[0] += -(-nbytes // 64) * 64
            assert top[0] <= nc.sbuf_usable_end, top
            return at

        def sb(name, shape, dt, at=None):
            size = int(np.prod(shape[1:])) * mybir.dt.size(dt)
            return nc.alloc_sbuf_tensor_at(name, shape, dt, offset=area(size) if at is None else at)

        KB = 1024
        a_stream = area(64 * KB)
        a_x = area(2 * KT * L * 4)
        a_y = area(32 * KB)
        a_m = area(32 * KB)
        a_head = area(NB * L * 4 + 10 * KB + 512)
        a_tmp = area(13 * KB)

        ident = sb("ident", [P, P], F32)
        par = sb("par", [P, 8, KT], F32)
        LN0G, LN0B, MHW, LN1G, LN1B, CONV = 0, 1, 2, 3, 4, 5

        raw = sb("raw", [P, CHUNKS, 4, GW], F32, a_stream)
        hi = sb("hi", [P, SLOT_N, 2, GW], F32R, a_stream + 32 * KB)
        lo = sb("lo", [P, SLOT_N, 2, GW], F32R, a_stream + 48 * KB)
        xh = sb("xh", [P, KT, L], F32R, a_x)
        xl = sb("xl", [P, KT, L], F32R, a_x + KT * L * 4)
        yh = sb("yh", [P, KT, SEQ], F32R, a_y)
        yl = sb("yl", [P, KT, SEQ], F32R, a_y + 16 * KB)
        neg_m = sb("neg_m", [P, HEADS, SEQ], F32, a_y + 16 * KB)
        mh = sb("mh", [P, KT, SEQ], F32R, a_m)
        ml = sb("ml", [P, KT, SEQ], F32R, a_m + 16 * KB)
        merged = sb("merged", [P, KT, SEQ], F32, a_m)
        hm_t = sb("hm_t", [P, KT, SEQ], F32, a_m + 16 * KB)
        tok = sb("tok", [P, 3, D], F32, a_m)
        qkv = sb("qkv", [P, NB, L], F32, a_head)
        at = a_head + NB * L * 4
        w_exp = sb("w_exp", [P, 640], F32, at)
        probs = sb("probs", [P, 640], F32, at + 2560)
        v_tok = sb("v_tok", [P, 3, HV + 1], F32, at + 5120)
        hm = sb("hm", [P, NT, HV], F32, at + 5120 + 3 * 257 * 4 + 20)
        LC = SEQ + CONV_W - 1
        t_cc = sb("t_cc", [P, NB, LC], F32, a_tmp)
        t_z = sb("t_z", [P, NB, LC], F32, a_tmp + NB * L * 4)
        t_y = sb("t_y", [P, NB, SEQ], F32, a_tmp + 2 * NB * L * 4)
        x32 = sb("x32", [P, 4, L], F32, a_tmp)
        gw = sb("gw", [P, KT, GCOLS], F32, a_tmp + NB * L * 4)
        sig = sb("sig", [P, NB, SEQ], F32, a_tmp)
        h1pre = sb("h1pre", [P, KT, SEQ], F32, a_y)
        xn1 = sb("xn1", [P, NT, D], F32, a_y + 16 * KB)
        h32 = sb("h32", [P, KT, SEQ], F32, a_y)
        hh1 = sb("hh1", [P, KT, SEQ], F32R, a_x)
        hl1 = sb("hl1", [P, KT, SEQ], F32R, a_x + KT * L * 4)
        h1 = sb("h1", [P, NT, D], F32, a_m)
        g1_bc = sb("g1_bc", [P, D], F32, a_m + 16 * KB)
        b1_bc = sb("b1_bc", [P, D], F32, a_m + 24 * KB)
        keys = sb("keys", [P, 2 * PH, P], F32, a_tmp + NB * SEQ * 4)
        keys_t = sb("keys_t", [P, 2 * PH, P], F32, a_head)
        qs = sb("qs", [P, NB, SEQ], F32, a_head + 8 * KB)
        sc_all = sb("sc_all", [P, NT * 2 * PH, NKEY], F32, a_y)
        u_rows = [sb(f"u_rows{j}", [P, D], F32, (a_m if j < 2 else a_y) + 16 * KB + (j % 2) * 8 * KB)
                  for j in range(RING)]
        v_rows = sb("v_rows", [P, RING, D], F32, a_stream)
        diag = sb("diag", [P, RING, P], F32, a_x)
        junk = sb("junk", [P, 2, D], BF16, a_tmp)
        tail = sb("tail", [P, TAIL_Q * 512], F32, a_tmp + 8 * KB)
        y2 = sb("y2", [P, NT, D], F32, a_x + 10 * KB)
        g2_bc = sb("g2_bc", [P, D], F32, a_stream + 32 * KB)
        b2_bc = sb("b2_bc", [P, D], F32, a_stream + 40 * KB)
        par_rows = sb("par_rows", [P, P], F32)
        bias_if = sb("bias_if", [P, 1], F32)
        g1 = sb("g1", [HEADS, L], F32, a_tmp)
        g2 = sb("g2", [HEADS, L], F32, a_tmp + 2 * KB)
        cum_f = sb("cum_f", [HEADS, L], F32, a_tmp + 4 * KB)
        run_m = sb("run_m", [HEADS, L], F32, a_tmp + 6 * KB)
        a_tok = sb("a_tok", [P, 3, HEADS], F32)
        em_tok = sb("em_tok", [P, NT, HEADS], F32)
        st = sb("st", [P, 3, 4, 6], F32)
        mv = sb("mv", [P, 3, 2], F32)
        rstd = sb("rstd", [P, 3], F32)
        nmr = sb("nmr", [P, 3], F32)
        m_half = sb("m_half", [P, 4], F32)
        den = sb("den", [P, 2], F32)
        rden = sb("rden", [P, 2], F32)
        ssq = sb("ssq", [P, 2], F32)
        ssn = sb("ssn", [P, 2], F32)
        rrms = sb("rrms", [P, 2], F32)
        hscale = sb("hscale", [P, 2], F32)
        alpha_i = sb("alpha_i", [P, P], F32)
        zeros = sb("zeros", [P, 512], BF16)
        iota16 = sb("iota16", [P, TOPK], F32)
        a_top = area(8 * KB)
        sel = sb("sel", [HEADS, HEADS, P], F32, a_top)
        li = sb("li", [HEADS, L], F32, a_top + 4 * KB)
        fp = sb("fp", [HEADS, L], F32, a_top + 4 * KB + L * 4)
        ones_row = sb("ones_row", [HEADS, L], F32, a_top + 4 * KB + 2 * L * 4)
        sc = sb("sc", [P, 2, NKEY], F32, a_top)
        scw = sb("scw", [P, 2, NKEY], F32, a_top + 1 * KB)
        cand = sb("cand", [P, TOPK, TOPK], F32, a_top + 2 * KB)
        candw = sb("candw", [P, TOPK, TOPK], F32, a_top + 3 * KB)
        oh = sb("oh", [P, 2, TOPK, TOPK], F32, a_top + 4 * KB)
        ohv = sb("ohv", [P, 2, TOPK, TOPK], F32, a_top + 6 * KB)
        kv = sb("kv", [P, 2, TOPK], F32)
        ki = sb("ki", [P, 2, TOPK], U32)
        kif = sb("kif", [P, 2, TOPK], F32)
        best = sb("best", [P, TOPK], F32)
        pos = sb("pos", [P, TOPK], U32)
        pos2 = sb("pos2", [P, 2, TOPK], U32)
        pos2f = sb("pos2f", [P, 2, TOPK], F32)
        eid = sb("eid", [P, 2, TOPK], F32)
        eidx = sb("eidx", [P, TOPK], F32)
        nbest = sb("nbest", [P, 1], F32)
        pe_ = sb("pexp", [P, TOPK], F32)
        psm = sb("psum_exp", [P, 1], F32)
        prs = sb("prs", [P, 1], F32)
        idx_all = sb("idx_all", [P, NT * SLOTS], U32)
        g_all = sb("g_all", [P, NT * SLOTS], F32)
        idx_u = sb("idx_u", [P, 2, TOPK], U32)
        idx_v = sb("idx_v", [P, 2, TOPK], U32)
        dots = sb("dots", [P, 2, TOPK], F32)
        gel = sb("gel", [P, 2, TOPK], F32)
        coef = sb("coef", [P, 2, TOPK], F32)

        ps = ctx.enter_context(nc.psum_tensor("ps", [P, 8, 512], F32))

        sems = {}

        def S(name):
            if name not in sems:
                sems[name] = ctx.enter_context(nc.semaphore(name))
            return sems[name]

        for n in ("set_apart rows_cleared tok_in0 tok_in1 tok_in2 par_in bif_in gw_in keys_in bc1_in bc2_in out_done "
                  "raw_in0 raw_in1 raw_in2 raw_in3 hi_ready lo_ready halves_used block_done "
                  "blocks_evacuated const_ready ln0_stats ln0_rstd ln0_nmr ln0_norm x_transposed x32_ready "
                  "x_split gate_w_used gates_read gate_mid gate_log gate_rows "
                  "gate_bc gate_bc_read pool_chain dve_chain act_chain par_done par_read args_ready "
                  "weights_ready masked v_transposed scores_done v_copied probs_ready num_done "
                  "recip_ready ssq_ready rms_ready hm_done hm_transposed hmt_written cc_ready sig_ready "
                  "m32_ready hi_part y_ready merged_ready h1pre_ready h1_transposed ln1_stats ln1_rstd "
                  "ln1_nmr xn1_ready xn1_transposed h32_ready h1t_ready h1_ready keys_transposed "
                  "keys_copied qk_done sc_copied topk_neg topk_exp topk_done u_in0 u_in1 u_in2 u_in3 "
                  "v_in0 v_in1 v_in2 v_in3 dots_done rows_added diag_ready gelu_ready coef_ready "
                  "ffn_done ln2_stats ln2_rstd ln2_nmr xn2_ready y2_ready tail_added").split():
            S(n)
        def set_apart(eng):
            eng.sem_inc(S("set_apart"), 1)

        raw_in = [S(f"raw_in{j}") for j in range(CHUNKS)]
        u_in = [S(f"u_in{j}") for j in range(RING)]
        v_in = [S(f"v_in{j}") for j in range(RING)]

        block = ctx.enter_context(nc.Block())
        XB = 3
        TOKR = [(0, META), (META, P), (META + P, P)]
        HCRED, BCRED = SLOT_N, NB

        @block.sync
        def _(sp):
            def load_group(G, sources):
                for j in range(CHUNKS):
                    if not (isinstance(G, int) and G == 0):
                        sp.wait_ge(S("lo_ready"), (G - 1) * HALVES + 2 * (j + 1))
                        set_apart(sp)
                    at = 0
                    for n, (w, c0, width) in enumerate(sources):
                        src = w[j * 4 * P:(j + 1) * 4 * P, bass.ds(c0, width)]
                        sp.dma_start(raw[:, j, :, at:at + width],
                                     src.rearrange("(k p) n -> p k n", p=P)).then_inc(raw_in[j], 16)
                        at += width

            sp.dma_start(tok[:META, 0, :], meta_tokens).then_inc(S("tok_in0"), 16)
            sp.dma_start(tok[:, 1, :], x[0, 0:P, :]).then_inc(S("tok_in1"), 16)
            sp.dma_start(tok[:, 2, :], x[0, P:2 * P, :]).then_inc(S("tok_in2"), 16)
            sp.wait_ge(S("rows_cleared"), 2)
            for n, v in enumerate((ln0_g, ln0_b, mh_norm_w[0], ln1_g[0], ln1_b[0])):
                sp.dma_start(par_rows[n * KT:(n + 1) * KT, :],
                             v.rearrange("(k p) -> k p", p=P)).then_inc(S("par_in"), 16)
            sp.dma_start(par_rows[CONV * KT:(CONV + CONV_W) * KT, :],
                         conv_w[0].rearrange("w (k p) -> (w k) p", p=P)).then_inc(S("par_in"), 16)
            for n in range(2):
                sp.dma_start(bias_if[n * GF:n * GF + HEADS, :], b_if[0, n * HEADS:(n + 1) * HEADS].rearrange("(h a) -> h a", a=1)
                             ).then_inc(S("bif_in"), 16)
            for n in range(2):
                src = w_in[:, C_GATE + n * HEADS:C_GATE + (n + 1) * HEADS]
                sp.dma_start(gw[:, :, n * GF:n * GF + HEADS], src.rearrange("(k p) n -> p k n", p=P)
                             ).then_inc(S("gw_in"), 16)

            def head_sources(h):
                return [(w_in, C_Q + h * HQK, HQK), (w_in, C_K + h * HQK, HQK), (w_in, C_V + h * HV, HV)]

            load_group(0, head_sources(0))
            with sp.Fori(1, HEADS) as h:
                load_group(h, head_sources(h))
            with sp.Fori(0, 4) as g:
                for s, c in enumerate((C_CC, C_CX, C_CB)):
                    load_group(g * 3 + (G_CONV + s), [(w_in, g * GW + c, GW)])
            with sp.Fori(0, 4) as g:
                load_group(g * 2 + G_GA, [(w_in, g * GW + C_GA, GW)])
                load_group(g * 2 + (G_GA + 1), [(p_a, g * GW, GW)])
            with sp.Fori(0, 4) as g:
                load_group(g + G_O, [(w_in, g * GW + C_O, GW)])
            with sp.Fori(0, 4) as g:
                load_group(g * 2 + G_GB, [(w_in, g * GW + C_GB, GW)])
                load_group(g * 2 + (G_GB + 1), [(p_b, g * GW, GW)])
            with sp.Fori(0, 4) as g:
                load_group(g + G_WO, [(w_o, g * GW, GW)])
            with sp.Fori(0, 4) as g:
                load_group(g + G_WQ, [(peer_wq, g * GW, GW)])
            sp.wait_ge(S("halves_used"), GROUPS * HALVES + HCRED)
            for t, v in ((g2_bc, ln2_g), (b2_bc, ln2_b)):
                sp.dma_start(t[:, :], v[0].partition_broadcast(P)).then_inc(S("bc2_in"), 16)
            for T in range(NT):
                for q in range(QN):
                    sp.wait_ge(S("y2_ready"), T * QN + q + 1)
                    sp.dma_start(out[0, T * P:(T + 1) * P, q * QW:(q + 1) * QW], y2[:, T, q * QW:(q + 1) * QW]
                                 ).then_inc(S("out_done"), 16)
            sp.wait_ge(S("out_done"), 16 * NT * QN)

        @block.tensor
        def _(pe):
            def mm(o, a, b, start, stop):
                return nc.tensor.matmul(o, a, b, start=start, stop=stop)

            def group(G, rh, rl, cols, after=None, before=None, bank=None):
                for hh in range(HALVES):
                    if before:
                        before(hh)
                    pe.wait_ge(S("hi_ready"), G * HALVES + (hh + 1))
                    pe.wait_ge(S("lo_ready"), G * HALVES + (hh + 1))
                    for nb in range(NB):
                        if hh == 0:
                            pe.wait_ge(S("blocks_evacuated"), G * NB + (nb + 1))
                            if bank:
                                bank(nb)
                        c0, c1 = cols(nb)
                        o = ps[:, nb, 0:c1 - c0]
                        for k2 in range(2):
                            kt = hh * 2 + k2
                            wh = hi[:, hh % SLOT_N, k2, nb * P:(nb + 1) * P]
                            wl = lo[:, hh % SLOT_N, k2, nb * P:(nb + 1) * P]
                            mm(o, wh, rh[:, kt, c0:c1], kt == 0, False)
                            mm(o, wh, rl[:, kt, c0:c1], False, False)
                            last = mm(o, wl, rh[:, kt, c0:c1], False, kt == KT - 1)
                        if nb == NB - 1:
                            last.then_inc(S("halves_used"), 1)
                        elif hh == HALVES - 1:
                            last.then_inc(S("block_done"), 1)
                    if after and hh in after:
                        after[hh]()

            conv = lambda nb: (META - CONV_W + 1, L)
            outs = lambda nb: (META, L)
            own = lambda nb: (0, SEQ)

            pe.sem_inc(S("halves_used"), HCRED)
            pe.sem_inc(S("blocks_evacuated"), BCRED)
            pe.sem_inc(S("hm_done"), 1)
            pe.sem_inc(S("hmt_written"), 2)

            pe.wait_ge(S("const_ready"), 1)
            pe.wait_ge(S("par_in"), 16 * 6)
            nc.tensor.transpose(ps[:, 0, 0:P], par_rows[:, :], ident[:, :]).then_inc(S("par_done"), 1)
            pe.wait_ge(S("ln0_norm"), 3)
            pe.wait_ge(S("gw_in"), 32)
            def x_block(kt):
                if kt >= XB:
                    pe.wait_ge(S("x32_ready"), kt - XB + 1)
                for n, (c0, cnt) in enumerate(TOKR):
                    last = nc.tensor.transpose(ps[:, 4 + kt % XB, c0:c0 + cnt], tok[:cnt, n, kt * P:(kt + 1) * P],
                                               ident[:cnt, :cnt])
                last.then_inc(S("x_transposed"), 1)

            def gate_block(k):
                pe.wait_ge(S("x32_ready"), k + 1)
                mm(ps[:GCOLS, 7, 0:L], gw[:, k, :], x32[:, k % 4, :], k == 0, k == KT - 1
                   ).then_inc(S("gate_w_used"), 1)

            def prologue(hh):
                for kt in range(2 * hh, 2 * hh + 2):
                    if kt + XB < KT:
                        x_block(kt + XB)
                    gate_block(kt)
                pe.wait_ge(S("x_split"), 2 * hh + 2)

            for kt in range(XB):
                x_block(kt)

            def gate_rows():
                pe.wait_ge(S("gate_rows"), 1)
                for n, (c0, cnt) in enumerate(TOKR):
                    nc.tensor.transpose(ps[:cnt, 4, n * HEADS:(n + 1) * HEADS], g1[:, c0:c0 + cnt],
                                        ident[:HEADS, :HEADS])
                for T in range(NT):
                    c0, cnt = TOKR[T + 1]
                    last = nc.tensor.transpose(ps[:cnt, 4, (3 + T) * HEADS:(4 + T) * HEADS], g2[:, c0:c0 + cnt],
                                               ident[:HEADS, :HEADS])
                last.then_inc(S("gate_bc"), 1)
                for r in range(2):
                    if r:
                        pe.wait_ge(S("gate_bc_read"), 2)
                    for h in range(4 * r, 4 * r + 4):
                        last = mm(ps[:, 5 + (h % 4) // 2, (h % 2) * SEQ:(h % 2 + 1) * SEQ], sel[:, h, :],
                                  run_m[:, META:L], True, True)
                    last.then_inc(S("gate_bc"), 1)

            def mlstm_scores(h):
                pe.wait_ge(S("blocks_evacuated"), h * NB + NB + BCRED)
                pe.wait_ge(S("hm_done"), h + 1)
                pe.wait_ge(S("hmt_written"), h * 2 + 2)
                for vb in range(2):
                    for n, (c0, cnt) in enumerate(TOKR):
                        o = ps[:cnt, 5, vb * P:(vb + 1) * P] if n == 0 else \
                            ps[:, 4, (n - 1) * HV + vb * P:(n - 1) * HV + (vb + 1) * P]
                        last = nc.tensor.transpose(o, qkv[:, 2 + vb, c0:c0 + cnt], ident[:, :])
                last.then_inc(S("v_transposed"), 1)
                mm(ps[:, 6, 0:SEQ], qkv[:, 1, META:META + P], qkv[:, 0, META:L], True, True)
                mm(ps[:META, 6, SEQ:2 * SEQ], qkv[:, 1, 0:META], qkv[:, 0, META:L], True, True)
                mm(ps[:, 7, 0:P], qkv[:, 1, META + P:L], qkv[:, 0, META + P:L], True, True
                   ).then_inc(S("scores_done"), 1)

            def mlstm_values(h):
                pe.wait_ge(S("probs_ready"), h + 1)
                pe.wait_ge(S("v_copied"), h * 2 + 2)
                mm(ps[:, 4, 0:HV + 1], probs[:, 0:P], v_tok[:, 0, :], True, False)
                mm(ps[:, 4, 0:HV + 1], probs[:META, 384:512], v_tok[:META, 2, :], False, True)
                mm(ps[:, 5, 0:HV + 1], probs[:, 256:384], v_tok[:, 0, :], True, False)
                mm(ps[:, 5, 0:HV + 1], probs[:, 128:256], v_tok[:, 1, :], False, False)
                mm(ps[:, 5, 0:HV + 1], probs[:META, 512:640], v_tok[:META, 2, :], False, True
                   ).then_inc(S("num_done"), 1)

            def mlstm_transpose(h):
                pe.wait_ge(S("hm_done"), h + 2)
                for vb in range(2):
                    for T in range(NT):
                        last = nc.tensor.transpose(ps[:, 6, vb * SEQ + T * P:vb * SEQ + (T + 1) * P],
                                                   hm[:, T, vb * P:(vb + 1) * P], ident[:, :])
                last.then_inc(S("hm_transposed"), 1)

            def mlstm(h):
                return {0: lambda: mlstm_scores(h), 4: lambda: mlstm_values(h), 7: lambda: mlstm_transpose(h)}

            head_cols = lambda nb: (META, L) if nb == 0 else (0, L)
            group(0, xh, xl, head_cols, before=prologue)
            def first_scores():
                pe.wait_ge(S("gate_bc_read"), 3)
                mlstm_scores(0)

            group(1, xh, xl, head_cols, {1: gate_rows, 4: first_scores, 6: lambda: mlstm_values(0),
                                         7: lambda: mlstm_transpose(0)})
            with pe.Fori(2, HEADS) as G:
                group(G, xh, xl, head_cols, mlstm(G - 1))
            group(G_CONV, xh, xl, conv, mlstm(HEADS - 1))
            group(G_CONV + 1, xh, xl, conv)
            group(G_CONV + 2, xh, xl, outs)
            with pe.Fori(1, 4) as g:
                group(g * 3 + G_CONV, xh, xl, conv)
                group(g * 3 + (G_CONV + 1), xh, xl, conv)
                group(g * 3 + (G_CONV + 2), xh, xl, outs)
            with pe.Fori(0, 4) as g:
                group(g * 2 + G_GA, xh, xl, outs)
                pe.wait_ge(S("y_ready"), 4)
                group(g * 2 + (G_GA + 1), yh, yl, own)
            with pe.Fori(0, 4) as g:
                group(g + G_O, xh, xl, outs)
            with pe.Fori(0, 4) as g:
                group(g * 2 + G_GB, xh, xl, outs)
                pe.wait_ge(S("y_ready"), 8)
                group(g * 2 + (G_GB + 1), yh, yl, own)
            def merged_wait(hh):
                if hh % 2 == 0:
                    pe.wait_ge(S("merged_ready"), hh // 2 + 1)

            with pe.Fori(0, 4) as g:
                group(g + G_WO, mh, ml, own, before=merged_wait)

            def key_blocks():
                pe.wait_ge(S("keys_in"), 16)
                for c in range(4):
                    if c >= 2:
                        pe.wait_ge(S("keys_copied"), c - 1)
                    for n in range(4):
                        last = nc.tensor.transpose(ps[:, 6 + c % 2, n * P:(n + 1) * P], keys[:, 4 * c + n, :],
                                                   ident[:, :])
                    last.then_inc(S("keys_transposed"), 1)

            pe.wait_ge(S("h1pre_ready"), KT)
            for T in range(NT):
                for kt in range(KT):
                    last = nc.tensor.transpose(ps[:, 4 * (1 - T) + kt // 4, (kt % 4) * P:(kt % 4 + 1) * P],
                                               h1pre[:, kt, T * P:(T + 1) * P], ident[:, :])
                last.then_inc(S("h1_transposed"), 1)
            for T in range(NT):
                pe.wait_ge(S("xn1_ready"), T + 1)
                for kt in range(KT):
                    last = nc.tensor.transpose(ps[:, 4 * (1 - T) + kt // 4, (kt % 4) * P:(kt % 4 + 1) * P],
                                               xn1[:, T, kt * P:(kt + 1) * P], ident[:, :])
                last.then_inc(S("xn1_transposed"), 2)

            def router_scores(g):
                pe.wait_ge(S("blocks_evacuated"), (G_WQ + g) * NB + NB + BCRED)
                if g:
                    pe.wait_ge(S("sc_copied"), NT * g)
                for T in range(NT):
                    for nb in range(NB):
                        last = mm(ps[:, 4 + T, nb * NKEY:(nb + 1) * NKEY], qs[:, nb, T * P:(T + 1) * P],
                                  keys_t[:, g * NB + nb, :], True, True)
                    last.then_inc(S("qk_done"), 1)

            def h1_wait(hh):
                if hh % 2 == 0:
                    pe.wait_ge(S("h1t_ready"), hh // 2 + 1)

            group(G_WQ, hh1, hl1, own, {5: key_blocks}, before=h1_wait,
                  bank=lambda nb: pe.wait_ge(S("h32_ready"), KT + 4 * (nb + 1)))
            for g in range(1, 4):
                group(G_WQ + g, hh1, hl1, own, {0: lambda: router_scores(g - 1)})
            router_scores(3)

            def tile_open(T):
                pe.wait_ge(S("h1_ready"), T + 1)
                for q in range(4):
                    mm(ps[:, 4 * T + q, :], alpha_i[:, :], h1[:, T, q * 512:(q + 1) * 512], True, False)

            def rows_wait(u, k):
                pe.wait_ge(v_in[k % RING], u * 64 + 16 * (k // RING + 1))
                pe.wait_ge(S("diag_ready"), u * TOPK + (k + 1))

            def row_product(T, k, q):
                return mm(ps[:, 4 * T + q, :], diag[:, k % RING, :], v_rows[:, k % RING, q * 512:(q + 1) * 512],
                          False, False)

            def close_bank(T, q):
                mm(ps[:, 4 * T + q, :], zeros[:, 0:P], zeros[:, :], False, True).then_inc(S("ffn_done"), 1)

            def add_rows(T, u, close=False):
                for k in range(TOPK):
                    rows_wait(u, k)
                    for q in range(4):
                        last = row_product(T, k, q)
                        if q == 3:
                            last.then_inc(S("rows_added"), 1)
                        if close and k == TOPK - 1:
                            close_bank(T, q)

            def add_last_rows(T, u):
                own_q = 4 - TAIL_Q
                for k in range(TOPK):
                    rows_wait(u, k)
                    for q in range(own_q):
                        last = row_product(T, k, q)
                        if q == own_q - 1:
                            last.then_inc(S("rows_added"), 1)
                        if k == TOPK - 1:
                            close_bank(T, q)
                pe.wait_ge(S("tail_added"), TOPK)
                for q in range(own_q, 4):
                    mm(ps[:, 4 * T + q, :], ident[:, :], tail[:, (q - own_q) * 512:(q - own_q + 1) * 512], False, False)
                    close_bank(T, q)

            pe.sem_inc(S("rows_added"), RING)
            tile_open(0)
            with pe.Fori(0, 3) as i:
                add_rows(0, i * 2)
                add_rows(0, i * 2 + 1)
            add_rows(0, 6)
            add_rows(0, 7, close=True)
            pe.wait_ge(S("sc_copied"), NT * 4)
            tile_open(1)
            with pe.Fori(4, 7) as i:
                add_rows(1, i * 2)
                add_rows(1, i * 2 + 1)
            add_rows(1, 14)
            add_last_rows(1, 15)

        @block.scalar
        def _(act):
            chain = Steps(act, S("act_chain"))

            def A(o, i, f, **kw):
                return nc.scalar.activation(o, i, f, **kw)

            def split_hi(G, hh, head):
                act.wait_ge(raw_in[hh // 2], G * 48 + 48 if head else G * 16 + 16 * (2 * HEADS + 1))
                act.wait_ge(S("halves_used"), G * HALVES + (hh + 1))
                A(hi[:, hh % SLOT_N, :, :], raw[:, hh // 2, 2 * (hh % 2):2 * (hh % 2) + 2, :], ACT.Copy
                  ).then_inc(S("hi_ready"), 1)

            def halves(G, after=None, head=False, head_next=False, last=False, first=AHEAD):
                for n in range(first, HALVES if last else HALVES + AHEAD):
                    if n < HALVES:
                        split_hi(G, n, head)
                    else:
                        split_hi(G + 1, n - HALVES, head_next)
                    if after and n in after:
                        after[n]()
                if last:
                    for n in sorted(after or {}):
                        if n >= HALVES:
                            after[n]()

            def block_wait(G, nb):
                if nb < NB - 1:
                    act.wait_ge(S("block_done"), G * (NB - 1) + (nb + 1))
                else:
                    act.wait_ge(S("halves_used"), G * HALVES + HALVES + HCRED)

            def evacuate(G, dst, c0, f=ACT.Copy):
                for nb in range(NB):
                    block_wait(G, nb)
                    A(dst(nb), ps[:, nb, 0:c0], f).then_inc(S("blocks_evacuated"), 1)

            for n, cnt in enumerate((META, P, P)):
                act.wait_ge(S("ln0_nmr"), n + 1)
                A(tok[:cnt, n, :], tok[:cnt, n, :], ACT.Identity, scale=rstd[:cnt, n:n + 1],
                  bias=nmr[:cnt, n:n + 1]).then_inc(S("ln0_norm"), 1)
            act.wait_ge(S("par_read"), 1)
            for kt in range(KT):
                if kt in FIRST_SPLITS:
                    split_hi(0, FIRST_SPLITS.index(kt), True)
                act.wait_ge(S("x_transposed"), kt + 1)
                if kt >= 4:
                    act.wait_ge(S("x_split"), kt - 3)
                    act.wait_ge(S("gate_w_used"), kt - 3)
                A(x32[:, kt % 4, :], ps[:, 4 + kt % XB, 0:L], ACT.Identity, scale=par[:, LN0G, kt:kt + 1],
                  bias=par[:, LN0B, kt:kt + 1]).then_inc(S("x32_ready"), 1)
            def gates_in():
                act.wait_ge(S("gate_w_used"), KT)
                act.wait_ge(S("bif_in"), 32)
                for n, t in enumerate((li, fp)):
                    A(t[:, :], ps[n * GF:n * GF + HEADS, 7, 0:L], ACT.Identity, bias=bias_if[n * GF:n * GF + HEADS, 0:1]
                      ).then_inc(S("gates_read"), 1)
                act.wait_ge(S("gate_mid"), 1)
                chain.link(A(g1[:, :], g1[:, :], ACT.Exp))
                A(g1[:, :], g1[:, :], ACT.Ln, bias=1.0).then_inc(S("gate_log"), 1)

            def gates_out():
                act.wait_ge(S("gate_bc"), 1)
                chain.link(A(a_tok[:META, 0, :], ps[:META, 4, 0:HEADS], ACT.Copy))
                chain.link(A(a_tok[:, 1:3, :], ps[:, 4, HEADS:3 * HEADS].rearrange("p (n h) -> p n h", n=2), ACT.Copy))
                A(em_tok[:, :, :], ps[:, 4, 3 * HEADS:5 * HEADS].rearrange("p (n h) -> p n h", n=2), ACT.Exp
                  ).then_inc(S("gate_bc_read"), 1)
                for r in range(2):
                    act.wait_ge(S("gate_bc"), 2 + r)
                    A(neg_m[:, 4 * r:4 * r + 4, :].rearrange("p (a b) t -> p a (b t)", a=2), ps[:, 5:7, :], ACT.Copy,
                      scale=-1.0).then_inc(S("gate_bc_read"), 1)

            def mlstm_copy_v(h):
                act.wait_ge(S("v_transposed"), h + 1)
                A(v_tok[:, 0:2, 0:HV], ps[:, 4, :].rearrange("p (n v) -> p n v", n=2), ACT.Copy).then_inc(S("v_copied"), 1)
                A(v_tok[:META, 2, 0:HV], ps[:META, 5, 0:HV], ACT.Copy).then_inc(S("v_copied"), 1)

            def mlstm_exp(h):
                act.wait_ge(S("args_ready"), h + 1)
                A(w_exp[:, 0:384], w_exp[:, 0:384], ACT.Exp)
                A(w_exp[:META, 384:640], w_exp[:META, 384:640], ACT.Exp).then_inc(S("weights_ready"), 1)

            def mlstm_square(h):
                act.wait_ge(S("recip_ready"), h + 1)
                for T in range(NT):
                    A(hm[:, T, :], ps[:, 4 + T, 0:HV], ACT.Square, scale=rden[:, T:T + 1],
                      accum_out=ssq[:, T:T + 1]).then_inc(S("ssq_ready"), 1)

            def mlstm_out(h):
                act.wait_ge(S("hm_transposed"), h + 1)
                for vb in range(2):
                    A(hm_t[:, bass.ds(h * 2 + vb, 1), :].rearrange("p a t -> p (a t)"),
                      ps[:, 6, vb * SEQ:(vb + 1) * SEQ], ACT.Copy).then_inc(S("hmt_written"), 1)

            def mlstm(h):
                return {4: lambda: mlstm_copy_v(h), 5: lambda: mlstm_exp(h), 9: lambda: mlstm_square(h)}

            to_qkv = lambda nb: qkv[:, nb, META:L] if nb == 0 else qkv[:, nb, :]

            def evacuate_head(G):
                for nb in range(NB):
                    block_wait(G, nb)
                    A(to_qkv(nb), ps[:, nb, 0:SEQ if nb == 0 else L], ACT.Copy).then_inc(S("blocks_evacuated"), 1)

            halves(0, head=True, head_next=True, first=len(FIRST_SPLITS))
            gates_in()
            evacuate_head(0)
            halves(1, {5: gates_out, 7: lambda: mlstm_copy_v(0), 8: lambda: mlstm_exp(0), 10: lambda: mlstm_square(0)},
                   head=True, head_next=True)
            act.wait_ge(S("scores_done"), 1)
            evacuate_head(1)
            mlstm_out(0)
            with act.Fori(2, HEADS - 1) as G:
                halves(G, mlstm(G - 1), head=True, head_next=True)
                act.wait_ge(S("scores_done"), G)
                evacuate_head(G)
                mlstm_out(G - 1)
            G = HEADS - 1
            halves(G, mlstm(G - 1), head=True)
            act.wait_ge(S("scores_done"), G)
            evacuate_head(G)
            mlstm_out(G - 1)

            def conv_groups(g, after=None):
                G = g * 3 + G_CONV
                halves(G, after)
                evacuate(G, lambda nb: t_cc[:, nb, :], LC)
                if after:
                    mlstm_out(HEADS - 1)
                halves(G + 1)
                halves(G + 2)
                act.wait_ge(S("m32_ready"), g + 1)
                A(yh[:, bass.ds(g * NB, NB), :], t_y[:, :, :], ACT.Copy).then_inc(S("hi_part"), 1)

            conv_groups(0, mlstm(HEADS - 1))
            with act.Fori(1, 4) as g:
                conv_groups(g)

            to_sig = lambda nb: sig[:, nb, :]
            with act.Fori(0, 4) as g:
                halves(g * 2 + G_GA)
                act.wait_ge(S("m32_ready"), g + 4)
                evacuate(g * 2 + G_GA, to_sig, SEQ, ACT.Sigmoid)
                halves(g * 2 + (G_GA + 1))
            with act.Fori(0, 4) as g:
                halves(g + G_O)
                act.wait_ge(S("m32_ready"), g + 8)
                evacuate(g + G_O, to_sig, SEQ, ACT.Sigmoid)
                act.wait_ge(S("m32_ready"), g + 9)
                A(yh[:, bass.ds(g * NB, NB), :], t_y[:, :, :], ACT.Copy).then_inc(S("hi_part"), 1)
            with act.Fori(0, 4) as g:
                halves(g * 2 + G_GB)
                act.wait_ge(S("m32_ready"), g + 12)
                evacuate(g * 2 + G_GB, to_sig, SEQ, ACT.Sigmoid)
                halves(g * 2 + (G_GB + 1))
                act.wait_ge(S("m32_ready"), g + 13)
                A(mh[:, bass.ds(g * NB, NB), :], t_y[:, :, :], ACT.Copy).then_inc(S("hi_part"), 1)
            with act.Fori(0, 4) as g:
                halves(g + G_WO)

            for T in range(NT):
                act.wait_ge(S("ln1_nmr"), T + 1)
                A(xn1[:, T, :].rearrange("p (a b) -> p a b", a=4), ps[:, 4 * (1 - T):4 * (2 - T), :], ACT.Identity,
                  scale=rstd[:, T:T + 1], bias=nmr[:, T:T + 1]).then_inc(S("xn1_ready"), 1)
            for T in range(NT):
                act.wait_ge(S("xn1_transposed"), 2 * (T + 1))
                for kt in range(KT):
                    A(h32[:, kt, T * P:(T + 1) * P], ps[:, 4 * (1 - T) + kt // 4, (kt % 4) * P:(kt % 4 + 1) * P],
                      ACT.Identity, scale=par[:, LN1G, kt:kt + 1], bias=par[:, LN1B, kt:kt + 1]
                      ).then_inc(S("h32_ready"), 1)

            def copy_scores(g):
                for T in range(NT):
                    act.wait_ge(S("qk_done"), NT * g + T + 1)
                    A(sc_all[:, T * 2 * PH + NB * g:T * 2 * PH + NB * (g + 1), :].rearrange("p a b -> p (a b)"), ps[:, 4 + T, :], ACT.Copy
                      ).then_inc(S("sc_copied"), 1)

            def softmax_exp(u):
                act.wait_ge(S("topk_neg"), u + 1)
                A(pe_[:, :], best[:, :], ACT.Exp, bias=nbest[:, 0:1], accum_out=psm[:, 0:1]
                  ).then_inc(S("topk_exp"), 1)

            def copy_keys():
                for c in range(4):
                    act.wait_ge(S("keys_transposed"), c + 1)
                    A(keys_t[:, 4 * c:4 * c + 4, :].rearrange("p a b -> p (a b)"), ps[:, 6 + c % 2, :], ACT.Copy
                      ).then_inc(S("keys_copied"), 1)

            def router_work(g):
                if g < 0:
                    return {8: copy_keys}
                if g:
                    return {6: lambda: copy_scores(g)}
                return {4: lambda: copy_scores(0), 5: lambda: softmax_exp(0), 9: lambda: softmax_exp(1)}

            act.wait_ge(S("h1t_ready"), 4)
            for g in range(4):
                halves(G_WQ + g, router_work(g - 1), last=g == 3)
                if g == 3:
                    break
                if g:
                    act.wait_ge(S("qk_done"), NT * g)
                evacuate(G_WQ + g, lambda nb: qs[:, nb, :], SEQ)
            act.wait_ge(S("qk_done"), NT * 3)
            evacuate(G_WQ + 3, lambda nb: qs[:, nb, :], SEQ)
            copy_scores(3)
            softmax_exp(2)

            def gelu(u, par_u):
                act.wait_ge(S("dots_done"), u * TOPK + (TOPK + RING))
                A(gel[:, par_u, :], dots[:, par_u, :], ACT.Gelu).then_inc(S("gelu_ready"), 1)

            def diagonals(u, par_u):
                act.wait_ge(S("coef_ready"), u + 1)
                for k in range(TOPK):
                    act.wait_ge(S("rows_added"), u * TOPK + (k + 1))
                    A(diag[:, k % RING, :], ident[:, :], ACT.Copy, scale=coef[:, par_u, k:k + 1]
                      ).then_inc(S("diag_ready"), 1)

            with act.Fori(0, 3) as i:
                for e in range(2):
                    u = i * 2 + (e + 1)
                    gelu(u - 1, e)
                    diagonals(u - 1, e)
                    softmax_exp(u + 2)
            for u in (7, 8):
                gelu(u - 1, (u - 1) % 2)
                diagonals(u - 1, (u - 1) % 2)
                softmax_exp(u + 2)

            def ln2(T):
                act.wait_ge(S("ln2_nmr"), T + 1)
                b = 4 // QN
                for q in range(QN):
                    A(y2[:, T, q * QW:(q + 1) * QW].rearrange("p (a b) -> p a b", a=b),
                      ps[:, 4 * T + q * b:4 * T + (q + 1) * b, :], ACT.Identity,
                      scale=rstd[:, T:T + 1], bias=nmr[:, T:T + 1]).then_inc(S("xn2_ready"), 1)

            with act.Fori(4, 6) as i:
                for e in range(2):
                    u = i * 2 + (e + 1)
                    gelu(u - 1, e)
                    diagonals(u - 1, e)
                    softmax_exp(u + 2)
            for u in (13, 14, 15, 16):
                gelu(u - 1, (u - 1) % 2)
                diagonals(u - 1, (u - 1) % 2)
                if u == 13:
                    softmax_exp(15)
                    ln2(0)
            ln2(1)

        @block.vector
        def _(dve):
            chain = Steps(dve, S("dve_chain"))
            V = nc.vector

            def split_lo(G, hh):
                dve.wait_ge(S("hi_ready"), G * HALVES + (hh + 1))
                V.tensor_tensor(lo[:, hh % SLOT_N, :, :], raw[:, hh // 2, 2 * (hh % 2):2 * (hh % 2) + 2, :],
                                hi[:, hh % SLOT_N, :, :].bitcast(F32), ALU.subtract).then_inc(S("lo_ready"), 1)

            def halves(G, after=None, last=False, first=AHEAD):
                for n in range(first, HALVES if last else HALVES + AHEAD):
                    split_lo(*((G, n) if n < HALVES else (G + 1, n - HALVES)))
                    if after and n in after:
                        after[n]()
                if last:
                    for n in sorted(after or {}):
                        if n >= HALVES:
                            after[n]()

            def block_wait(G, nb):
                if nb < NB - 1:
                    dve.wait_ge(S("block_done"), G * (NB - 1) + (nb + 1))
                else:
                    dve.wait_ge(S("halves_used"), G * HALVES + HALVES + HCRED)

            def blk(t, g, nb):
                return t[:, bass.ds(g * NB + nb, 1), :].rearrange("p a t -> p (a t)")

            def res(t, g, nb):
                return t[:, bass.ds(g * NB + nb, 1), META:L].rearrange("p a t -> p (a t)").bitcast(F32)

            def stats(src, n, cnt, done, piece_wait=None):
                for q in range(4):
                    if piece_wait:
                        piece_wait(q)
                    ins = V.bn_stats(st[:cnt, n, q, :], src(q))
                chain.link(ins)
                chain.link(V.bn_aggr(mv[:cnt, n, :], st[:cnt, n, :, :].rearrange("p a b -> p (a b)")))
                V.tensor_scalar(rstd[:cnt, n:n + 1], mv[:cnt, n, 1:2], EPS, None, ALU.add).then_inc(S(done), 1)

            def neg_mean(n, cnt, done):
                V.scalar_tensor_tensor(nmr[:cnt, n:n + 1], mv[:cnt, n, 0:1], -1.0, rstd[:cnt, n:n + 1],
                                       ALU.mult, ALU.mult).then_inc(S(done), 1)

            V.memset(ones_row[:, :], 1.0)
            V.memset(gw[:, :, :], 0.0).then_inc(S("rows_cleared"), 1)
            V.memset(par_rows[:, :], 0.0).then_inc(S("rows_cleared"), 1)
            for n, cnt in enumerate((META, P, P)):
                dve.wait_ge(S(f"tok_in{n}"), 16)
                stats(lambda q: tok[:cnt, n, q * 512:(q + 1) * 512], n, cnt, "ln0_stats")
            for n, cnt in enumerate((META, P, P)):
                dve.wait_ge(S("ln0_rstd"), n + 1)
                neg_mean(n, cnt, "ln0_nmr")
            dve.wait_ge(S("par_done"), 1)
            V.tensor_copy(par[:, :, :].rearrange("p a b -> p (a b)"), ps[:, 0, 0:P]).then_inc(S("par_read"), 1)
            V.memset(v_tok[:, :, HV:HV + 1], 1.0)
            for kt in range(KT):
                if kt in FIRST_SPLITS:
                    split_lo(0, FIRST_SPLITS.index(kt))
                dve.wait_ge(S("x32_ready"), kt + 1)
                chain.link(V.tensor_copy(xh[:, kt, :], x32[:, kt % 4, :]))
                V.tensor_tensor(xl[:, kt, :], x32[:, kt % 4, :], xh[:, kt, :].bitcast(F32), ALU.subtract
                                ).then_inc(S("x_split"), 1)
            def gates():
                dve.wait_ge(S("gates_read"), 2)
                V.scalar_tensor_tensor(g1[:, :], fp[:, :], -1.0, fp[:, :], ALU.mult, ALU.min).then_inc(S("gate_mid"), 1)
                chain.link(V.tensor_scalar(g2[:, :], fp[:, :], 0.0, None, ALU.min))
                dve.wait_ge(S("gate_log"), 1)
                chain.link(V.tensor_tensor(g2[:, :], g2[:, :], g1[:, :], ALU.subtract))
                chain.link(V.tensor_tensor_scan(cum_f[:, :], ones_row[:, :], g2[:, :], 0.0, ALU.mult, ALU.add))
                chain.link(V.tensor_tensor(g1[:, :], li[:, :], cum_f[:, :], ALU.subtract))
                chain.link(V.tensor_tensor_scan(run_m[:, :], g1[:, :], g1[:, :], 0.0, ALU.max, ALU.max))
                V.scalar_tensor_tensor(g2[:, :], cum_f[:, :], -1.0, run_m[:, :], ALU.mult, ALU.subtract
                                       ).then_inc(S("gate_rows"), 1)

            two = lambda ap: ap.rearrange("p (a b) -> p a b", b=P)
            w_diag0 = lambda t: t[:, 0:512].rearrange("p (a b) -> p a b", b=256)[:, :, 0:P]

            def hrow(t, h, c0, c1, cnt=P):
                return t[:cnt, bass.ds(h, 1), c0:c1].rearrange("p a t -> p (a t)")

            def acol(n, h, cnt=P):
                return a_tok[:cnt, n, bass.ds(h, 1)]

            def mlstm_args(h):
                V.tensor_scalar(w_diag0(w_exp), two(hrow(neg_m, h, 0, SEQ)), acol(1, h), 0.0, ALU.add, ALU.min)
                V.tensor_scalar(w_exp[:, P:2 * P], hrow(neg_m, h, P, SEQ), acol(2, h), 0.0, ALU.add, ALU.min)
                V.tensor_scalar(w_exp[:META, 384:640], hrow(neg_m, h, 0, SEQ, META), acol(0, h, META), 0.0,
                                ALU.add, ALU.min).then_inc(S("args_ready"), 1)

            def mlstm_probs(h):
                dve.wait_ge(S("scores_done"), h + 1)
                dve.wait_ge(S("masked"), h + 1)
                V.scalar_tensor_tensor(w_diag0(probs), two(ps[:, 6, 0:SEQ]), QSCALE, w_diag0(w_exp), ALU.mult, ALU.mult)
                V.scalar_tensor_tensor(probs[:, P:2 * P], ps[:, 7, 0:P], QSCALE, w_exp[:, P:2 * P], ALU.mult, ALU.mult)
                V.scalar_tensor_tensor(probs[:META, 384:640], ps[:META, 6, SEQ:2 * SEQ], QSCALE,
                                       w_exp[:META, 384:640], ALU.mult, ALU.mult).then_inc(S("probs_ready"), 1)

            def mlstm_den(h):
                dve.wait_ge(S("num_done"), h + 1)
                for T in range(NT):
                    ins = V.tensor_scalar(den[:, T:T + 1], ps[:, 4 + T, HV:HV + 1], -1.0, em_tok[:, T, bass.ds(h, 1)],
                                          ALU.mult, ALU.max)
                chain.link(ins)
                for T in range(NT):
                    ins = V.scalar_tensor_tensor(den[:, T:T + 1], ps[:, 4 + T, HV:HV + 1], 1.0, den[:, T:T + 1],
                                                 ALU.mult, ALU.max)
                chain.link(ins)
                V.reciprocal(rden[:, :], den[:, :]).then_inc(S("recip_ready"), 1)

            def mlstm_norm(h):
                dve.wait_ge(S("rms_ready"), h + 1)
                chain.link(V.tensor_tensor(hscale[:, :], rden[:, :], rrms[:, :], ALU.mult))
                V.tensor_scalar(hm[:, 0, :], ps[:, 4, 0:HV], hscale[:, 0:1], None, ALU.mult)
                V.tensor_scalar(hm[:, 1, :], ps[:, 5, 0:HV], hscale[:, 1:2], None, ALU.mult).then_inc(S("hm_done"), 1)

            def mlstm(h):
                return {4: lambda: mlstm_args(h), 6: lambda: mlstm_probs(h), 8: lambda: mlstm_den(h),
                        10: lambda: mlstm_norm(h)}

            def first_args():
                dve.wait_ge(S("gate_bc_read"), 3)
                mlstm_args(0)

            halves(0, first=len(FIRST_SPLITS))
            gates()
            halves(1, {6: first_args, 8: lambda: mlstm_probs(0), 9: lambda: mlstm_den(0), 10: lambda: mlstm_norm(0)})
            with dve.Fori(2, HEADS) as G:
                chain.loop(G - 2, 3)
                halves(G, mlstm(G - 1))
                chain.end(HEADS - 2)

            def conv_groups(g, after=None):
                G = g * 3 + G_CONV
                halves(G, after)
                halves(G + 1)
                for nb in range(NB):
                    block_wait(G + 1, nb)
                    ins = V.tensor_tensor(t_z[:, nb, :], ps[:, nb, 0:LC], t_cc[:, nb, :], ALU.mult)
                    ins.then_inc(S("blocks_evacuated"), 1)
                w = lambda k, nb: par[:, CONV + k, bass.ds(g * NB + nb, 1)]
                dve.wait_ge(S("blocks_evacuated"), G * NB + (2 * NB + BCRED))
                for nb in range(NB):
                    ins = V.tensor_scalar(t_y[:, nb, :], t_z[:, nb, 0:SEQ], w(0, nb), None, ALU.mult)
                chain.link(ins)
                for k in (1, 2):
                    for nb in range(NB):
                        ins = V.scalar_tensor_tensor(t_y[:, nb, :], t_z[:, nb, k:SEQ + k], w(k, nb),
                                                     t_y[:, nb, :], ALU.mult, ALU.add)
                    chain.link(ins)
                halves(G + 2)
                for nb in range(NB):
                    block_wait(G + 2, nb)
                    V.tensor_tensor(t_y[:, nb, :], ps[:, nb, 0:SEQ], t_y[:, nb, :], ALU.mult
                                    ).then_inc(S("blocks_evacuated"), 1)
                dve.wait_ge(S("blocks_evacuated"), G * NB + (3 * NB + BCRED))
                dve.sem_inc(S("m32_ready"), 1)
                dve.wait_ge(S("hi_part"), g + 1)
                V.tensor_tensor(yl[:, bass.ds(g * NB, NB), :], t_y[:, :, :], yh[:, bass.ds(g * NB, NB), :].bitcast(F32),
                                ALU.subtract).then_inc(S("y_ready"), 1)

            conv_groups(0, mlstm(HEADS - 1))
            with dve.Fori(1, 4) as g:
                chain.loop(g - 1, 3)
                conv_groups(g)
                chain.end(3)

            with dve.Fori(0, 4) as g:
                halves(g * 2 + G_GA)
                halves(g * 2 + (G_GA + 1))
                for nb in range(NB):
                    block_wait(g * 2 + (G_GA + 1), nb)
                    V.tensor_tensor(blk(merged, g, nb), ps[:, nb, 0:SEQ], sig[:, nb, :], ALU.mult
                                    ).then_inc(S("blocks_evacuated"), 1)
                dve.wait_ge(S("blocks_evacuated"), g * 2 * NB + ((G_GA + 2) * NB + BCRED))
                dve.sem_inc(S("m32_ready"), 1)
            with dve.Fori(0, 4) as g:
                halves(g + G_O)
                chain.loop(g, 1)
                dve.wait_ge(S("blocks_evacuated"), g * NB + ((G_O + 1) * NB + BCRED))
                for nb in range(NB):
                    ins = V.scalar_tensor_tensor(t_y[:, nb, :], sig[:, nb, :], par[:, MHW, bass.ds(g * NB + nb, 1)],
                                                 blk(hm_t, g, nb), ALU.mult, ALU.mult)
                chain.link(ins)
                dve.sem_inc(S("m32_ready"), 1)
                dve.wait_ge(S("hi_part"), g + 5)
                V.tensor_tensor(yl[:, bass.ds(g * NB, NB), :], t_y[:, :, :], yh[:, bass.ds(g * NB, NB), :].bitcast(F32),
                                ALU.subtract).then_inc(S("y_ready"), 1)
                chain.end(4)
            with dve.Fori(0, 4) as g:
                halves(g * 2 + G_GB)
                halves(g * 2 + (G_GB + 1))
                chain.loop(g, 1)
                for nb in range(NB):
                    block_wait(g * 2 + (G_GB + 1), nb)
                    V.tensor_tensor(t_y[:, nb, :], ps[:, nb, 0:SEQ], sig[:, nb, :], ALU.mult
                                    ).then_inc(S("blocks_evacuated"), 1)
                dve.wait_ge(S("blocks_evacuated"), g * 2 * NB + ((G_GB + 2) * NB + BCRED))
                chain.link(V.tensor_tensor(t_y[:, :, :], t_y[:, :, :], merged[:, bass.ds(g * NB, NB), :], ALU.add))
                dve.sem_inc(S("m32_ready"), 1)
                dve.wait_ge(S("hi_part"), g + 9)
                V.tensor_tensor(ml[:, bass.ds(g * NB, NB), :], t_y[:, :, :], mh[:, bass.ds(g * NB, NB), :].bitcast(F32),
                                ALU.subtract).then_inc(S("merged_ready"), 1)
                chain.end(4)
            with dve.Fori(0, 4) as g:
                halves(g + G_WO)
                chain.loop(g, 1)
                for nb in range(NB):
                    block_wait(g + G_WO, nb)
                    ins = V.scalar_tensor_tensor(blk(h1pre, g, nb), res(xh, g, nb), ALPHA, ps[:, nb, 0:SEQ],
                                                 ALU.mult, ALU.add)
                    ins.then_inc(S("blocks_evacuated"), 1)
                dve.wait_ge(S("blocks_evacuated"), g * NB + ((G_WO + 1) * NB + BCRED))
                chain.link(V.memset(nbest[:, :], 0.0))
                for nb in range(NB):
                    V.scalar_tensor_tensor(blk(h1pre, g, nb), res(xl, g, nb), ALPHA, blk(h1pre, g, nb),
                                           ALU.mult, ALU.add).then_inc(S("h1pre_ready"), 1)
                chain.end(4)

            for T in range(NT):
                dve.wait_ge(S("h1_transposed"), T + 1)
                stats(lambda q: ps[:, 4 * (1 - T) + q, :], T, P, "ln1_stats")
            for T in range(NT):
                dve.wait_ge(S("ln1_rstd"), T + 1)
                neg_mean(T, P, "ln1_nmr")
            for c in range(4):
                dve.wait_ge(S("h32_ready"), KT + 4 * (c + 1))
                chain.link(V.tensor_copy(hh1[:, 4 * c:4 * c + 4, :], h32[:, 4 * c:4 * c + 4, :]))
                V.tensor_tensor(hl1[:, 4 * c:4 * c + 4, :], h32[:, 4 * c:4 * c + 4, :],
                                hh1[:, 4 * c:4 * c + 4, :].bitcast(F32), ALU.subtract).then_inc(S("h1t_ready"), 1)

            def topk(u, scores):
                def step(ins):
                    chain.link(ins)
                    set_apart(dve)

                step(V.tensor_copy(sc[:, :, :], scores))
                for p in range(2):
                    ins = V.max(kv[:, p, 0:8], sc[:, p, :])
                step(ins)
                for p in range(2):
                    V.max_index(ki[:, p, 0:8], kv[:, p, 0:8], sc[:, p, :])
                    ins = V.match_replace(scw[:, p, :], kv[:, p, 0:8], sc[:, p, :], NEG)
                step(ins)
                for p in range(2):
                    ins = V.max(kv[:, p, 8:16], scw[:, p, :])
                step(ins)
                for p in range(2):
                    ins = V.max_index(ki[:, p, 8:16], kv[:, p, 8:16], scw[:, p, :])
                step(ins)
                V.tensor_copy(kif[:, :, :], ki[:, :, :])
                step(V.tensor_tensor(cand[:, :, :], kv[:, 0, :].unsqueeze(2).to_broadcast([P, TOPK, TOPK]),
                                           kv[:, 1, :].unsqueeze(1).to_broadcast([P, TOPK, TOPK]), ALU.add))
                flat = lambda t: t[:, :, :].rearrange("p a b -> p (a b)")
                step(V.max(best[:, 0:8], flat(cand)))
                V.max_index(pos[:, 0:8], best[:, 0:8], flat(cand))
                step(V.match_replace(flat(candw), best[:, 0:8], flat(cand), NEG))
                step(V.max(best[:, 8:16], flat(candw)))
                step(V.max_index(pos[:, 8:16], best[:, 8:16], flat(candw)))
                V.tensor_scalar(nbest[:, :], best[:, 0:1], -1.0, None, ALU.mult).then_inc(S("topk_neg"), 1)
                V.tensor_scalar(pos2[:, 0, :], pos[:, :], 4, None, ALU.logical_shift_right)
                step(V.tensor_scalar(pos2[:, 1, :], pos[:, :], TOPK - 1, None, ALU.bitwise_and))
                step(V.tensor_copy(pos2f[:, :, :], pos2[:, :, :]))
                for p in range(2):
                    ins = V.tensor_tensor(oh[:, p, :, :], pos2f[:, p, :].unsqueeze(2).to_broadcast([P, TOPK, TOPK]),
                                          iota16[:, :].unsqueeze(1).to_broadcast([P, TOPK, TOPK]), ALU.is_equal)
                step(ins)
                for p in range(2):
                    ins = V.tensor_tensor(ohv[:, p, :, :], oh[:, p, :, :],
                                          kif[:, p, :].unsqueeze(1).to_broadcast([P, TOPK, TOPK]), ALU.mult)
                step(ins)
                step(V.tensor_reduce(eid[:, :, :], ohv[:, :, :, :], AX.X, ALU.add))
                step(V.scalar_tensor_tensor(eidx[:, :], eid[:, 0, :], float(NKEY), eid[:, 1, :], ALU.mult, ALU.add))
                step(V.tensor_copy(idx_all[:, bass.ds(u * TOPK, TOPK)], eidx[:, :]))
                dve.wait_ge(S("topk_exp"), u + 1)
                step(V.reciprocal(prs[:, :], psm[:, :]))
                V.tensor_scalar(g_all[:, bass.ds(u * TOPK, TOPK)], pe_[:, :], prs[:, 0:1], None, ALU.mult
                                ).then_inc(S("topk_done"), 1)

            TOPK_LINKS = 18

            def scores_of(u):
                return sc_all[:, bass.ds(u * 2, 2), :]

            def dot(T, u, par_u, k):
                dve.wait_ge(u_in[k % RING], u * 64 + 16 * (k // RING + 1))
                dve.wait_ge(S("dots_done"), u * TOPK + (k + RING - 1))
                V.scalar_tensor_tensor(junk[:, k % 2, :], u_rows[k % RING][:, :], 1.0, h1[:, T, :], ALU.mult,
                                       ALU.mult, accum_out=dots[:, par_u, k:k + 1]).then_inc(S("dots_done"), 1)

            first_dots = list(range(TOPK))

            def first_topk(e):
                def f():
                    if e == 0:
                        dve.wait_ge(S("sc_copied"), NT)
                    topk(e, scores_of(e))
                return f

            def first_dot():
                dot(0, 0, 0, first_dots.pop(0))

            dve.wait_ge(S("const_ready"), 1)
            dve.sem_inc(S("dots_done"), RING)
            halves(G_WQ)
            halves(G_WQ + 1, {4: first_topk(0), 8: first_topk(1)})
            dve.wait_ge(S("h1_ready"), 1)
            halves(G_WQ + 2, {n: first_dot for n in range(AHEAD, AHEAD + HALVES)})
            halves(G_WQ + 3, {n: first_dot for n in range(AHEAD, HALVES)}, last=True)
            while first_dots:
                first_dot()
            dve.wait_ge(S("sc_copied"), NT * 4)
            topk(2, scores_of(2))

            def coefs(u, par_u):
                dve.wait_ge(S("gelu_ready"), u + 1)
                V.tensor_tensor(coef[:, par_u, :], gel[:, par_u, :], g_all[:, bass.ds(u * TOPK, TOPK)], ALU.mult
                                ).then_inc(S("coef_ready"), 1)

            def unit(T, u, par_u, after=None):
                for k in range(TOPK):
                    dot(T, u, par_u, k)
                    if k == 0:
                        coefs(u - 1, 1 - par_u)
                    if after and k in after:
                        after[k]()

            with dve.Fori(0, 3) as i:
                chain.loop(i, 2 * TOPK_LINKS)
                for e in range(2):
                    unit(0, i * 2 + (e + 1), 1 - e)
                    topk(i * 2 + (e + 3), scores_of(i * 2 + (e + 3)))
                chain.end(3)
            unit(0, 7, 1)
            topk(9, scores_of(9))
            dve.wait_ge(S("h1_ready"), 2)
            unit(1, 8, 0)
            topk(10, scores_of(10))

            def ln2_stats(T):
                stats(lambda q: ps[:, 4 * T + q, :], T, P, "ln2_stats",
                      lambda q: dve.wait_ge(S("ffn_done"), T * 4 + q + 1))

            def ln2_mean(T):
                dve.wait_ge(S("ln2_rstd"), T + 1)
                neg_mean(T, P, "ln2_nmr")

            def ln2_params(T, q):
                c = slice(q * QW, (q + 1) * QW)
                dve.wait_ge(S("bc2_in"), 32)
                dve.wait_ge(S("xn2_ready"), T * QN + q + 1)
                chain.link(V.tensor_tensor(y2[:, T, c], y2[:, T, c], g2_bc[:, c], ALU.mult))
                V.tensor_tensor(y2[:, T, c], y2[:, T, c], b2_bc[:, c], ALU.add).then_inc(S("y2_ready"), 1)

            with dve.Fori(4, 6) as i:
                chain.loop(i - 4, 2 * TOPK_LINKS)
                for e in range(2):
                    unit(1, i * 2 + (e + 1), 1 - e)
                    topk(i * 2 + (e + 3), scores_of(i * 2 + (e + 3)))
                chain.end(2)
            unit(1, 13, 1, {2: lambda: ln2_stats(0)})
            ln2_mean(0)
            topk(15, scores_of(15))
            unit(1, 14, 0, {4 * q + 4: lambda q=q: ln2_params(0, q) for q in range(QN)})
            unit(1, 15, 1)
            coefs(15, 1)
            dve.wait_ge(S("coef_ready"), 16)
            for k in range(TOPK):
                dve.wait_ge(v_in[k % RING], 15 * 64 + 16 * (k // RING + 1))
                row = v_rows[:, k % RING, D - TAIL_Q * 512:D]
                if k == 0:
                    V.tensor_scalar(tail[:, :], row, coef[:, 1, 0:1], None, ALU.mult).then_inc(S("tail_added"), 1)
                else:
                    dve.wait_ge(S("tail_added"), k)
                    V.scalar_tensor_tensor(tail[:, :], row, coef[:, 1, k:k + 1], tail[:, :], ALU.mult, ALU.add
                                           ).then_inc(S("tail_added"), 1)
            ln2_stats(1)
            ln2_mean(1)
            for q in range(QN):
                ln2_params(1, q)

        @block.gpsimd
        def _(pool):
            chain = Steps(pool, S("pool_chain"))
            Q = nc.gpsimd
            chain.link(Q.memset(ident[:, :], 0.0))
            chain.link(Q.affine_select(out=ident[:, :], in_=ident[:, :], compare_op=ALU.not_equal, fill=1.0, base=0,
                                       pattern=[[-1, P]], channel_multiplier=1))
            chain.link(Q.memset(alpha_i[:, :], 0.0))
            chain.link(Q.affine_select(out=alpha_i[:, :], in_=alpha_i[:, :], compare_op=ALU.not_equal, fill=ALPHA,
                                       base=0, pattern=[[-1, P]], channel_multiplier=1))
            chain.link(Q.memset(sel[:, :, :], 0.0))
            chain.link(Q.affine_select(out=sel[:, :, :], in_=sel[:, :, :], compare_op=ALU.not_equal, fill=1.0, base=0,
                                       pattern=[[-1, HEADS], [0, P]], channel_multiplier=1))
            chain.link(Q.memset(zeros[:, :], 0.0))
            chain.link(Q.memset(m_half[:, :], -0.5))
            Q.iota(iota16[:, :], [[1, TOPK]], base=0, channel_multiplier=0, allow_small_or_imprecise_dtypes=True
                   ).then_inc(S("const_ready"), 1)

            def rsqrt(name, n, cnt, count):
                pool.wait_ge(S(name + "_stats"), count)
                Q.tensor_tensor(rstd[:cnt, n:n + 1], rstd[:cnt, n:n + 1], m_half[:cnt, 0:1], ALU.pow
                                ).then_inc(S(name + "_rstd"), 1)

            for n, cnt in enumerate((META, P, P)):
                rsqrt("ln0", n, cnt, n + 1)

            def mlstm(h):
                pool.wait_ge(S("weights_ready"), h + 1)
                set_apart(pool)
                blocks = w_exp[:, 0:2 * P].rearrange("p (a b) -> p a b", b=P)
                Q.affine_select(out=blocks, in_=blocks, compare_op=ALU.is_ge, fill=0.0, base=0,
                                pattern=[[0, 2], [1, P]], channel_multiplier=-1).then_inc(S("masked"), 1)
                pool.wait_ge(S("ssq_ready"), h * 2 + 2)
                set_apart(pool)
                chain.link(Q.tensor_scalar(ssn[:, :], ssq[:, :], 1.0 / HV, EPS, ALU.mult, ALU.add))
                Q.tensor_tensor(rrms[:, :], ssn[:, :], m_half[:, 0:2], ALU.pow).then_inc(S("rms_ready"), 1)

            with pool.Fori(0, HEADS) as h:
                chain.loop(h, 1)
                mlstm(h)
                chain.end(HEADS)

            pool.wait_ge(S("merged_ready"), 4)
            pool.dma_start(keys[:, :, :], keys_rows).then_inc(S("keys_in"), 16)
            pool.wait_ge(S("h1pre_ready"), KT)
            for t, v in ((g1_bc, ln1_g), (b1_bc, ln1_b)):
                pool.dma_start(t[:, :], v[0].partition_broadcast(P)).then_inc(S("bc1_in"), 16)
            for T in range(NT):
                rsqrt("ln1", T, P, T + 1)
            pool.wait_ge(S("bc1_in"), 32)
            for T in range(NT):
                pool.wait_ge(S("xn1_ready"), T + 1)
                chain.link(Q.tensor_tensor(h1[:, T, :], xn1[:, T, :], g1_bc[:, :], ALU.mult))
                Q.tensor_tensor(h1[:, T, :], h1[:, T, :], b1_bc[:, :], ALU.add).then_inc(S("h1_ready"), 1)

            def stage(dst, u, par_u):
                pool.wait_ge(S("topk_done"), u + 1)
                set_apart(pool)
                chain.link(Q.tensor_copy(dst[:, par_u, :], idx_all[:, bass.ds(u * TOPK, TOPK)]))

            def gather_u(u, par_u, k):
                pool.wait_ge(S("dots_done"), u * TOPK + (k + 1))
                set_apart(pool)
                Q.indirect_dma_start(u_rows[k % RING][:, :], None, peer_u,
                                     bass.IndirectOffsetOnAxis(ap=idx_u[:, par_u, k:k + 1], axis=0)
                                     ).then_inc(u_in[k % RING], 16)

            def gather_v(u, par_u, k):
                pool.wait_ge(S("rows_added"), u * TOPK + (k + 1))
                set_apart(pool)
                Q.indirect_dma_start(v_rows[:, k % RING, :], None, peer_v,
                                     bass.IndirectOffsetOnAxis(ap=idx_v[:, par_u, k:k + 1], axis=0)
                                     ).then_inc(v_in[k % RING], 16)

            def unit(u, par_u, after=None):
                for k in range(TOPK):
                    if after and k in after:
                        after[k]()
                    if k == TOPK // 2:
                        if not isinstance(u, int) or u < 15:
                            stage(idx_u, u + 1, 1 - par_u)
                            set_apart(pool)
                        stage(idx_v, u, par_u)
                    gather_u(u, par_u, k)
                    gather_v(u - 1, 1 - par_u, k)

            pool.wait_ge(S("h1_ready"), NT)
            pool.wait_ge(S("xn1_transposed"), 2 * NT)
            stage(idx_u, 0, 0)
            for k in range(TOPK):
                gather_u(0, 0, k)
            stage(idx_u, 1, 1)
            stage(idx_v, 0, 0)
            pool.wait_ge(S("halves_used"), GROUPS * HALVES + HCRED)
            with pool.Fori(0, 3) as i:
                chain.loop(i, 4)
                for e in range(2):
                    unit(i * 2 + (e + 1), 1 - e)
                chain.end(3)
            unit(7, 1)
            unit(8, 0)
            with pool.Fori(4, 6) as i:
                chain.loop(i - 4, 4)
                for e in range(2):
                    unit(i * 2 + (e + 1), 1 - e)
                chain.end(2)
            unit(13, 1, {12: lambda: rsqrt("ln2", 0, P, 1)})
            unit(14, 0)
            unit(15, 1)
            for k in range(TOPK):
                if k >= RING:
                    pool.wait_ge(S("tail_added"), k - RING + 1)
                gather_v(15, 1, k)
            rsqrt("ln2", 1, P, 2)


_INS = ["x", "meta_tokens", "ln0_g", "ln0_b", "w_in", "b_if", "conv_w", "mh_norm_w", "p_a", "p_b", "w_o",
        "ln1_g", "ln1_b", "peer_wq", "peer_keys", "peer_u", "peer_v", "ln2_g", "ln2_b"]


def kernel(**inputs):
    import numpy as _np
    import concourse.bacc as _bacc
    from concourse import mybir as _mybir
    from concourse.bass_utils import run_bass_kernel_spmd as _run

    nc = _bacc.Bacc("TRN2", target_bir_lowering=False, num_devices=1)
    arrays, args = {}, []
    for name in _INS:
        a = _np.ascontiguousarray(inputs[name])
        arrays[f"in_{name}"] = a
        args.append(nc.dram_tensor(f"in_{name}", a.shape, _mybir.dt.from_np(a.dtype), kind="ExternalInput").ap())
    args.append(nc.dram_tensor("out_0", (1, SEQ, D), F32, kind="ExternalOutput").ap())
    decoder_layer(nc, *args)
    r = _run(nc, [arrays], core_ids=[0])
    return r.results[0]["out_0"]
```
